# Optimizing a Trainium2 kernel written in Bass

```python
import jax, jax.numpy as jnp
from jax import lax
import numpy as np

D_MODEL = 1024
BATCH = 1
SEQ = 256
DEPTH = 1

CHUNK = 64
MIX_WIDTH = D_MODEL
HGRN_WIDTH = MIX_WIDTH // 2
HGRN_HEAD_DIM = 128
HGRN_HEADS = HGRN_WIDTH // HGRN_HEAD_DIM
POOL_WIDTH = MIX_WIDTH - HGRN_WIDTH
POOL_WINDOWS = (2, 4, 8, 16)
N_POOL_GROUPS = len(POOL_WINDOWS)
POOL_GW = POOL_WIDTH // N_POOL_GROUPS
IN_COLS = 4 * HGRN_WIDTH + POOL_WIDTH
N_EXPERTS = 32
TOP_K = 4
D_FF = D_MODEL
SWIGLU_LIMIT = 7.0
SWIGLU_ALPHA = 1.702
EXPERT_BLOCK = 256
NORM_EPS = 1e-6

kernel_name = 'hybrid_hgrn2_pool_moe'

def rmsnorm(x, g):
    xf = x.astype(jnp.float32)
    y = xf * lax.rsqrt(jnp.mean(xf * xf, axis=-1, keepdims=True) + NORM_EPS)
    return (y * g.astype(jnp.float32)).astype(x.dtype)

def hgrn2(q_pre, f_pre, v, g_pre, lb, norm_g):
    B_, S_, _ = q_pre.shape
    n_chunks = S_ // CHUNK
    q = jax.nn.silu(q_pre.astype(jnp.float32))
    f = lb + (1.0 - lb) * jax.nn.sigmoid(f_pre.astype(jnp.float32))
    log_f = jnp.log(f)
    k = 1.0 - f

    def to_chunks(a):
        a = a.astype(jnp.float32).reshape(B_, n_chunks, CHUNK, HGRN_HEADS, HGRN_HEAD_DIM)
        return a.transpose(1, 0, 3, 2, 4)

    causal = jnp.tril(jnp.ones((CHUNK, CHUNK), dtype=bool))

    def step(state, inp):
        qc, kc, vc, lfc = inp
        b = jnp.cumsum(lfc, axis=2)
        b_last = b[:, :, -1, :]
        o_inter = jnp.einsum('bhtk,bhkv->bhtv', qc * jnp.exp(b), state)
        diff = b[:, :, :, None, :] - b[:, :, None, :, :]
        decay = jnp.exp(jnp.where(causal[None, None, :, :, None], diff, -jnp.inf))
        scores = jnp.einsum('bhtk,bhtsk,bhsk->bhts', qc, decay, kc)
        o = o_inter + jnp.einsum('bhts,bhsv->bhtv', scores, vc)
        new_state = jnp.exp(b_last)[..., None] * state + jnp.einsum(
            'bhsk,bhsv->bhkv', kc * jnp.exp(b_last[:, :, None, :] - b), vc)
        return new_state, o

    state0 = jnp.zeros((B_, HGRN_HEADS, HGRN_HEAD_DIM, HGRN_HEAD_DIM), jnp.float32)
    _, o = lax.scan(step, state0, (to_chunks(q), to_chunks(k), to_chunks(v), to_chunks(log_f)))
    o = o.transpose(1, 0, 3, 2, 4).reshape(B_, S_, HGRN_HEADS, HGRN_HEAD_DIM)
    o = o * lax.rsqrt(jnp.mean(o * o, axis=-1, keepdims=True) + NORM_EPS) * norm_g.astype(jnp.float32)
    gate = jax.nn.silu(g_pre.astype(jnp.float32)).reshape(B_, S_, HGRN_HEADS, HGRN_HEAD_DIM)
    return (o * gate).reshape(B_, S_, HGRN_WIDTH).astype(q_pre.dtype)

def pool_mixer(u, w, scale):
    B_, S_, _ = u.shape
    ug = u.astype(jnp.float32).reshape(B_, S_, N_POOL_GROUPS, POOL_GW)
    cs = jnp.cumsum(ug, axis=1)
    pos = jnp.arange(1, S_ + 1, dtype=jnp.float32)[None, :, None]
    outs = []
    for gi, win in enumerate(POOL_WINDOWS):
        c = cs[:, :, gi, :]
        lower = jnp.pad(c, ((0, 0), (win, 0), (0, 0)))[:, :S_]
        mean = (c - lower) / jnp.minimum(pos, float(win))
        outs.append(mean - ug[:, :, gi, :])
    d = jnp.stack(outs, axis=2)
    y = jnp.einsum('bsgc,gcd->bsgd', d, w.astype(jnp.float32))
    return (y.reshape(B_, S_, POOL_WIDTH) * scale.astype(jnp.float32)).astype(u.dtype)

def moe(h, w_r, b_r, w_g, b_g, w_u, b_u, w_d, b_d):
    B_, S_, D = h.shape
    N = B_ * S_
    t = h.reshape(N, D)
    logits = (t @ w_r + b_r).astype(jnp.float32)
    top_logit, top_e = lax.top_k(logits, TOP_K)
    gate = jax.nn.softmax(top_logit, axis=-1)
    M = N * TOP_K
    e_flat = top_e.reshape(M)
    order = jnp.argsort(e_flat)
    e_sorted = e_flat[order]
    tok_sorted = (order // TOP_K).astype(jnp.int32)
    gate_sorted = gate.reshape(M)[order]
    counts = jnp.bincount(e_flat, length=N_EXPERTS)
    start = jnp.cumsum(counts) - counts
    padded = (counts + EXPERT_BLOCK - 1) // EXPERT_BLOCK * EXPERT_BLOCK
    pad_end = jnp.cumsum(padded)
    pad_start = pad_end - padded
    dest = pad_start[e_sorted] + (jnp.arange(M) - start[e_sorted])
    P = M + N_EXPERTS * EXPERT_BLOCK
    n_blocks = P // EXPERT_BLOCK
    row_tok = jnp.full((P,), N, jnp.int32).at[dest].set(tok_sorted)
    row_gate = jnp.zeros((P,), jnp.float32).at[dest].set(gate_sorted)
    blk_e = jnp.minimum(jnp.searchsorted(pad_end, jnp.arange(n_blocks) * EXPERT_BLOCK, side='right'),
                        N_EXPERTS - 1)
    t_pad = jnp.concatenate([t, jnp.zeros((1, D), t.dtype)], axis=0)
    xs = t_pad[row_tok].reshape(n_blocks, EXPERT_BLOCK, D)

    def expert_block(args):
        xb, e = args
        gt = jnp.minimum(xb @ w_g[e] + b_g[e], SWIGLU_LIMIT)
        up = jnp.clip(xb @ w_u[e] + b_u[e], -SWIGLU_LIMIT, SWIGLU_LIMIT)
        act = (up + 1.0) * (gt * jax.nn.sigmoid(SWIGLU_ALPHA * gt))
        return act @ w_d[e] + b_d[e]

    ys = lax.map(expert_block, (xs, blk_e)).reshape(P, D)
    ys = ys * row_gate.astype(ys.dtype)[:, None]
    out = jax.ops.segment_sum(ys, row_tok, num_segments=N + 1)[:N]
    return out.reshape(B_, S_, D)

def setup_inputs(seed: int = 0) -> dict:
    key = jax.random.key(seed)
    ks = jax.random.split(key, 20)

    def nrm(k, shape, scale):
        return jax.random.normal(k, shape, jnp.float32) * scale

    return {
        'x': nrm(ks[0], (BATCH, SEQ, D_MODEL), 1.0),
        'norm1_g': 1.0 + nrm(ks[1], (DEPTH, D_MODEL), 0.02),
        'w_in': nrm(ks[2], (DEPTH, D_MODEL, IN_COLS), D_MODEL ** -0.5),
        'hgrn_lb': nrm(ks[3], (DEPTH + 1, HGRN_WIDTH), 0.5),
        'hgrn_norm_g': 1.0 + nrm(ks[4], (DEPTH, HGRN_HEAD_DIM), 0.02),
        'pool_w': nrm(ks[5], (DEPTH, N_POOL_GROUPS, POOL_GW, POOL_GW), POOL_GW ** -0.5),
        'pool_scale': 1.0 + nrm(ks[6], (DEPTH, POOL_WIDTH), 0.02),
        'w_out': nrm(ks[7], (DEPTH, MIX_WIDTH, D_MODEL), MIX_WIDTH ** -0.5),
        'norm2_g': 1.0 + nrm(ks[8], (DEPTH, D_MODEL), 0.02),
        'router_w': nrm(ks[9], (DEPTH, D_MODEL, N_EXPERTS), D_MODEL ** -0.5),
        'router_b': nrm(ks[10], (DEPTH, N_EXPERTS), 0.01),
        'w_gate': nrm(ks[11], (DEPTH, N_EXPERTS, D_MODEL, D_FF), D_MODEL ** -0.5),
        'b_gate': nrm(ks[12], (DEPTH, N_EXPERTS, D_FF), 0.01),
        'w_up': nrm(ks[13], (DEPTH, N_EXPERTS, D_MODEL, D_FF), D_MODEL ** -0.5),
        'b_up': nrm(ks[14], (DEPTH, N_EXPERTS, D_FF), 0.01),
        'w_down': nrm(ks[15], (DEPTH, N_EXPERTS, D_FF, D_MODEL), D_FF ** -0.5),
        'b_down': nrm(ks[16], (DEPTH, N_EXPERTS, D_MODEL), 0.01),
        'norm_f_g': 1.0 + nrm(ks[17], (D_MODEL,), 0.02),
    }

def reference(x, norm1_g, w_in, hgrn_lb, hgrn_norm_g, pool_w, pool_scale, w_out, norm2_g,
              router_w, router_b, w_gate, b_gate, w_up, b_up, w_down, b_down, norm_f_g):
    lb_all = jnp.cumsum(jax.nn.softmax(hgrn_lb.astype(jnp.float32), axis=0), axis=0)
    split_at = [HGRN_WIDTH, 2 * HGRN_WIDTH, 3 * HGRN_WIDTH, 4 * HGRN_WIDTH]
    for l in range(DEPTH):
        h = rmsnorm(x, norm1_g[l])
        proj = h @ w_in[l]
        q_pre, f_pre, v_in, g_pre, u_pool = jnp.split(proj, split_at, axis=-1)
        o_rec = hgrn2(q_pre, f_pre, v_in, g_pre, lb_all[l], hgrn_norm_g[l])
        o_pool = pool_mixer(u_pool, pool_w[l], pool_scale[l])
        x = x + jnp.concatenate([o_rec, o_pool], axis=-1) @ w_out[l]
        h = rmsnorm(x, norm2_g[l])
        x = x + moe(h, router_w[l], router_b[l], w_gate[l], b_gate[l], w_up[l], b_up[l],
                    w_down[l], b_down[l])
    return rmsnorm(x, norm_f_g)


_drawn_inputs = setup_inputs


def setup_inputs(seed=0):
    import zlib

    import numpy as np

    out = dict(_drawn_inputs(seed))
    spreads = {}
    factors = {'b_gate': 8.0, 'b_up': 21.642, 'b_down': 8.0, 'norm_f_g': 8.307}
    for name, (base, spread) in spreads.items():
        noise = np.random.default_rng([zlib.crc32(name.encode()), seed]).standard_normal(out[name].shape)
        drawn = base * np.exp(spread * noise) if base else spread * noise
        out[name] = __import__('jax').numpy.asarray(drawn.astype(out[name].dtype))
    for name, factor in factors.items():
        out[name] = (out[name] * factor).astype(out[name].dtype)
    return out
```

```python
from contextlib import ExitStack

import numpy as np

import concourse.bass as bass
from concourse import mybir

ALU = mybir.AluOpType
ACT = mybir.ActivationFunctionType
AX = mybir.AxisListType
F32 = mybir.dt.float32
I32 = mybir.dt.int32
U32 = mybir.dt.uint32

P = 128
D = 1024
SEQ = 256
T = SEQ // P
KC = D // P
HALF = 512
NH = D // HALF
HEADS = 4
CHUNK = 64
LEVELS = (128, 64, 32, 16, 8, 4, 2, 1)
SMALL = 32
WINDOWS = (2, 4, 8, 16)
E = 32
TOPK = 4
SLOTS = 64
PASSES = SEQ // SLOTS
PAIRS = E // 2
BODIES = PAIRS // 2
ROWS = 2
RING = 16
QUARTERS = KC // ROWS
CPP = 3 * QUARTERS * 2
FRONT = 14
AHEAD = 1
LIMIT = 7.0
ALPHA = 1.702
EPS = 1e-6
TAB = PASSES * E + 2


def layer_constants():
    t = np.arange(P)
    parts = {
        "ident": np.eye(P),
        "before": (t[:, None] < t[None, :]) * 1.0,
        "ones": np.ones((P, P)),
        "slot": np.tile(np.arange(SLOTS), (P, 1)),
        "expert": np.tile(np.arange(E), (P, 1)),
    }
    s, u = t[:, None] % SMALL, np.arange(SMALL)[None, :]
    masks = [(s // h % 2 == 0) & (u // h == s // h + 1) for h in LEVELS if h < SMALL] + [s == u]
    parts["masks"] = np.concatenate(masks, 1)
    w = max(WINDOWS)
    parts["short"] = np.tile(np.concatenate([n / np.minimum(np.arange(1, w + 1), n) for n in WINDOWS]), (P, 1))
    at, cols = {}, 0
    for k, a in parts.items():
        at[k] = (cols, a.shape[1])
        cols += a.shape[1]
    return np.concatenate([a.astype(np.float32) for a in parts.values()], 1), at


def hybrid_hgrn2_pool_moe(nc, A, out):
    _, const_at = layer_constants()
    w_in = A["w_in"][0].rearrange("(c p) n -> p c n", p=P)
    w_out = A["w_out"][0].rearrange("(c p) n -> p c n", p=P)
    x_dram = A["x"][0].rearrange("(t p) d -> p t d", p=P)
    out_dram = out[0].rearrange("(t p) d -> p t d", p=P)

    with ExitStack() as ctx:
        sems = {}

        def sem(name):
            if name not in sems:
                sems[name] = ctx.enter_context(nc.semaphore(name))
            return sems[name]

        def sb(name, shape, dt=F32):
            return ctx.enter_context(nc.sbuf_tensor(name, shape, dt))

        bank = [ctx.enter_context(nc.psum_tensor(f"bank{i}", [P, HALF], F32)) for i in range(8)]

        ring = sb("ring", [P, RING, ROWS, D])
        x = sb("x", [P, T, D])
        hn = sb("hn", [P, T, D])
        consts = sb("consts", [P, sum(n for _, n in const_at.values())])
        work = sb("work", [P, 12800])

        table_zeros = sb("zeros", [P, P])
        which_rows = sb("which", [E, 2, P])

        at = [0]

        def view(n):
            at[0] += n
            return work[:, at[0] - n:at[0]]

        hT = view(KC * SEQ).rearrange("p (c t) -> p c t", c=KC)
        vv = view(T * HALF).rearrange("p (t n) -> p t n", t=T)
        scT = view(HEADS * T * P).rearrange("p (a t) -> p a t", t=P)
        scX = view(HEADS * P).rearrange("p (h t) -> p h t", t=P)
        fs = view(HEADS * SEQ)
        ks = view(HEADS * SEQ)
        bs = view(HEADS * SEQ)
        qs = view(HEADS * SEQ)
        lv = [view(HEADS * SEQ) for _ in range(4)]
        gg = fs.rearrange("p (t n) -> p t n", t=T)
        picked = work[:, 2048 + 1024 + 1024 + 512 + 1024:][:, 0:6 * 256].rearrange("p (l x) -> p l x", l=6)
        ob = qs.rearrange("p (t n) -> p t n", t=T)
        osq = lv[0].rearrange("p (t n) -> p t n", t=T)
        sigg = lv[1].rearrange("p (t n) -> p t n", t=T)
        ocT = work[:, at[0] - 2048:at[0]].rearrange("p (c t) -> p c t", c=KC)
        uu = hn[:, 0, :].rearrange("p (g t) -> p g t", g=HEADS)
        cs = hn[:, 1, :].rearrange("p (g t) -> p g t", g=HEADS)
        at[0] = 0
        xsT = [view(KC * P).rearrange("p (c s) -> p c s", c=KC) for _ in range(2)]
        bias = view(3 * D).rearrange("p (m n) -> p m n", m=3)
        at[0] = 2048 + 3584
        gt, sg, up, yy, normf = (view(D) for _ in range(5))
        actT = view(D).rearrange("p (c s) -> p c s", c=KC)
        gtT = view(T * P)
        pick = view(T * P).rearrange("p (t s) -> p t s", t=T)
        pickg = view(T * P).rearrange("p (t s) -> p t s", t=T)
        assert at[0] <= 12800

        which = which_rows[:]
        zeros = table_zeros[:]

        def small(name, n, dt=F32):
            return sb(name, [P, n], dt)

        g1, g2 = small("g1", KC), small("g2", KC)
        lbr = sb("lbr", [P, 2, HEADS])
        lb, oml = small("lb", HEADS), small("oml", HEADS)
        pool_w = sb("pool_w_sb", [P, HEADS, P])
        pool_s, hnorm = small("pool_s", HEADS), small("hnorm", 1)
        router = sb("router", [P, KC, E])
        rbias = small("rbias", E)
        ss, ms, rstd, expo = small("ss", 8), small("ms", 8), small("rstd", 8), small("expo", 8)
        expo2 = small("expo2", 8)
        ssb, rstdb, rstdc = small("ssb", 4), small("rstdb", 2), small("rstdc", 2)
        ssc, msb, msc = small("ssc", 4), small("msb", 2), small("msc", 2)
        two = small("two", HEADS)
        logits = sb("logits", [P, T, E])
        top = sb("top", [P, T, 8])
        topi = sb("topi", [P, T, 8], U32)
        topf = sb("topf", [P, T * TOPK])
        ntop, psum_, rps = small("ntop", T), small("psum_", T), small("rps", T)
        prob = sb("prob", [P, T, TOPK])
        hit = sb("hit", [P, T * TOPK, E])
        hitg = sb("hitg", [P, T * TOPK, E])
        chosen = sb("chosen", [P, T, E])
        posn = sb("posn", [P, T, E])
        table = sb("table", [P, 2 * T, TAB])
        cur = sb("cur", [P, 2 * T, 2])
        most = small("most", 1)
        flag = sb("flag", [P, 1], I32)

        def const(name):
            a, n = const_at[name]
            return consts[:, a:a + n]

        ident, before, ones = const("ident"), const("before"), const("ones")
        slot_no, expert_no = const("slot"), const("expert")
        masks = const("masks").rearrange("p (l t) -> p l t", t=SMALL)
        short = const("short").rearrange("p (g t) -> p g t", g=len(WINDOWS))

        landed = [sem(f"landed{s}") for s in range(RING)]
        ring_read = sem("ring_read")

        def slot_of(i, j):
            return (FRONT + CPP * i + j) % RING

        def landed_at(n, i, j):
            turns = (FRONT + CPP * i + j) // RING + (slot_of(i, j) >= FRONT)
            return 16 * turns + n * (16 * 2 * CPP // RING)

        def w_out_half(s):
            return ring[:, 2 * s:2 * s + 2].rearrange("p s c n -> p (s c) n")

        def front_block(s):
            return ring[:, 2 * s:2 * s + 2].rearrange("p s c n -> p (s c n)").rearrange("p (c n) -> p c n", c=KC)

        def overflowed(eng):
            eng.wait_ge(sem("flag_ready"), 1)
            return eng.value_load(flag[0:1, 0:1], min_val=0, max_val=1)

        def product_done(eng, name, b, s):
            if b == 0:
                eng.wait_ge(sem(name), 1)
            else:
                eng.wait_ge(ring_read, AHEAD + 2 * s + 2)

        def lvl(b, half):
            return b.rearrange("p (n two h) -> p n two h", two=2, h=half)

        block = ctx.enter_context(nc.Block())

        @block.sync
        def _(sp):
            for t in range(T):
                sp.dma_start(x[:, t, :], x_dram[:, t, :]).then_inc(sem(f"x_in{t}"), 16)
            for s, col in enumerate((1, 0, 2, 4, 3)):
                if s:
                    sp.dma_start(front_block(s), w_in[:, :, col * HALF:(col + 1) * HALF]).then_inc(sem(f"front_in{s}"), 16)
                    continue
                for h in range(2):
                    r = slice(h * HALF // 2, (h + 1) * HALF // 2)
                    sp.dma_start(front_block(s)[:, :, r],
                                 w_in[:, :, col * HALF:(col + 1) * HALF][:, :, r]).then_inc(sem(f"front_in0_{h}"), 16)
            for s, h in ((5, 1), (6, 0)):
                sp.dma_start(w_out_half(s), w_out[:, 4 * h:4 * h + 4, :]).then_inc(sem(f"front_in{s}"), 16)

            def load(n, i, pair):
                p = n * 2 + i
                for j in range(CPP):
                    w = A[("w_gate", "w_up", "w_down")[j // (2 * QUARTERS)]]
                    c = ROWS * (j % (2 * QUARTERS) // 2)
                    e = sp.snap(pair * 2 + j % 2)
                    src = w[0, e].rearrange("(c p) n -> p c n", p=P)[:, c:c + ROWS, :]
                    sp.wait_ge(ring_read, AHEAD + p * CPP + j)
                    sp.dma_start(ring[:, slot_of(i, j)], src).then_inc(landed[slot_of(i, j)], 16)

            with sp.Fori(0, BODIES) as n:
                for i in range(2):
                    load(n, i, n * 2 + i)
            over = overflowed(sp)
            with sp.If(over > 0):
                with sp.Fori(1, PASSES) as c:
                    with sp.Fori(0, BODIES) as n:
                        for i in range(2):
                            load(c * BODIES + n, i, n * 2 + i)
            for t in range(T):
                for nh in range(NH):
                    r = slice(nh * HALF, (nh + 1) * HALF)
                    sp.wait_ge(sem("out_ready"), T * t + nh + 1)
                    sp.dma_start(out_dram[:, t, r], x[:, t, r]).then_inc(sem("out_sent"), 16)
            sp.wait_ge(sem("out_sent"), 16 * T * NH)

        @block.gpsimd
        def _(pool):
            pool.memset(expo[:], -0.5).then_inc(sem("expo_set"), 1)
            pool.memset(zeros, 0.0).then_inc(sem("zeros_set"), 1)
            pool.memset(scT, 0.0).then_inc(sem("scT_zero"), 1)
            pool.memset(lv[3], 1.0).then_inc(sem("resets"), 1)
            pool.wait_ge(sem("resets"), 1)
            pool.memset(lv[3].rearrange("p (n c) -> p n c", c=CHUNK)[:, :, 0:1], 0.0).then_inc(sem("resets"), 1)
            pool.memset(table[:], -1.0).then_inc(sem("table_set"), 1)
            pool.wait_ge(sem("expo_set"), 1)

            def rsqrt(o, i, n, name):
                for t in range(T):
                    pool.wait_ge(sem(f"{name}_mean"), t + 1)
                    pool.tensor_tensor(o[:, n * t:n * (t + 1)], i[:, n * t:n * (t + 1)], expo[:, 0:n],
                                       ALU.pow).then_inc(sem(f"{name}_rstd"), 1)

            rsqrt(rstd, ms, 1, "norm1")
            rsqrt(rstd, ms, HEADS, "head")
            rsqrt(rstdb, msb, 1, "norm2")
            rsqrt(rstdc, msc, 1, "normf")

        @block.scalar
        def _(act):
            def dma(dst, src, name):
                act.dma_start(dst, src, allow_slow_non_contiguous=True).then_inc(sem(name), 16)

            dma(consts[:, 0:P], A["consts"][:, 0:P], "ident_in")
            dma(g1[:], A["norm1_g"][0].rearrange("(c p) -> p c", p=P), "g1_in")
            for r in range(2):
                dma(lbr[:, r, :], A["hgrn_lb"][r].rearrange("(c p) -> p c", p=P), "lb_in")
            act.wait_ge(sem("expo_set"), 1)
            act.activation(expo2[:], expo[:], ACT.Square).then_inc(sem("squared"), 1)
            for t in range(T):
                act.wait_ge(sem(f"x_in{t}"), 16)
                act.activation(lv[t], x[:, t, :], ACT.Square, accum_out=ss[:, t:t + 1]).then_inc(sem("norm1_sum"), 1)
            act.wait_ge(sem("lb_diff"), 1)
            act.activation(lb[:], two[:], ACT.Sigmoid).then_inc(sem("lb_ready"), 1)
            dma(consts[:, P:], A["consts"][:, P:], "consts_in")
            dma(pool_w[:], A["pool_w"][0].rearrange("g c d -> c g d"), "rest_in")
            dma(pool_s[:], A["pool_scale"][0].rearrange("(c p) -> p c", p=P), "rest_in")
            dma(hnorm[:], A["hgrn_norm_g"].rearrange("o p -> p o"), "rest_in")
            dma(g2[:], A["norm2_g"][0].rearrange("(c p) -> p c", p=P), "rest_in")
            dma(router[:], A["router_w"][0].rearrange("(c p) e -> p c e", p=P), "rest_in")
            dma(rbias[:], A["router_b"].to_broadcast([P, E]), "rest_in")
            for b in range(2):
                product_done(act, "f_done", b, 0)
                act.activation(fs[:, b * HALF:(b + 1) * HALF], bank[4 + b][:], ACT.Sigmoid).then_inc(sem("f_sig"), 1)
            act.wait_ge(sem("k_ready"), 1)
            act.activation(fs, fs, ACT.Ln).then_inc(sem("logf_ready"), 1)
            for b in range(2):
                product_done(act, "q_done", b, 1)
                act.activation(lv[0][:, b * HALF:(b + 1) * HALF], bank[6 + b][:], ACT.Sigmoid).then_inc(sem("q_sig"), 1)

            def level_exp(n):
                act.wait_ge(sem("diff_ready"), n + 1)
                act.activation(lv[n % 4], lv[n % 4], ACT.Exp).then_inc(sem("decay_ready"), 1)

            for n in range(4):
                level_exp(n)
            for t in range(T):
                product_done(act, "v_done", t, 2)
                act.copy(vv[:, t, :], bank[t][:]).then_inc(sem("v_ready"), 1)
            for n in range(4, 6):
                level_exp(n)
            act.wait_ge(sem("scored"), 3)
            act.copy(scX.rearrange("p h t -> p (h t)"), bank[4][:]).then_inc(sem("coarse_ready"), 1)
            act.wait_ge(sem("scT_zero"), 1)
            act.copy(scT[0:64, :, 64:128], bank[5][0:64, :].rearrange("p (a t) -> p a t", a=8)).then_inc(sem("coarse_ready"), 1)
            for a in range(2):
                act.copy(scT[64 * a:64 * a + 32, :, 64 * a + 32:64 * a + 64],
                         bank[6][64 * a:64 * a + 32, 0:256].rearrange("p (a t) -> p a t", a=8)).then_inc(sem("coarse_ready"), 1)
            for n in range(6, 8):
                level_exp(n)
            for b in range(2):
                product_done(act, "u_done", b, 3)
                act.copy(uu[:, 2 * b:2 * b + 2, :], bank[2 + b][:].rearrange("p (g t) -> p g t", g=2)).then_inc(sem("u_ready"), 1)
            for t in range(T):
                product_done(act, "g_done", t, 4)
                act.activation(sigg[:, t, :], bank[t][:], ACT.Sigmoid).then_inc(sem("g_sig"), 1)
            act.wait_ge(sem("rest_in"), 96)
            for g in range(HEADS):
                act.wait_ge(sem("pool_done"), g // 2 + 1)
                act.activation(ocT[:, HEADS + g, :], bank[2 + g // 2][:, g % 2 * SEQ:(g % 2 + 1) * SEQ], ACT.Copy,
                               scale=pool_s[:, g:g + 1]).then_inc(sem("pooled_ready"), 1)
            for t in range(T):
                act.wait_ge(sem("o_done"), t + 1)
                act.activation(osq[:, t, :], bank[6 + t][:], ACT.Square).then_inc(sem("o_squares"), 1)
            for h in range(HEADS):
                act.wait_ge(sem("oT_done"), h // 2 + 1)
                act.activation(ocT[:, h, :], bank[4 + h // 2][:, h % 2 * SEQ:(h % 2 + 1) * SEQ], ACT.Copy,
                               scale=hnorm[:, 0:1]).then_inc(sem("heads_ready"), 1)

            for m, name in enumerate(("b_gate", "b_up", "b_down")):
                dma(bias[0:E, m, :], A[name][0], "bias_in")
            for q in range(T * NH):
                act.wait_ge(sem("mixed"), q + 1)
                r = slice(q % NH * HALF, (q % NH + 1) * HALF)
                act.activation(lv[q // NH][:, r], x[:, q // NH, r], ACT.Square,
                               accum_out=ssb[:, q:q + 1]).then_inc(sem("norm2_sum"), 1)
                if q % NH:
                    t = q // NH
                    act.wait_ge(sem("norm2_rstd"), t + 1)
                    act.activation(hn[:, t, :], x[:, t, :], ACT.Copy, scale=rstdb[:, t:t + 1]).then_inc(sem("rows_ready"), 1)
            for t in range(T):
                act.wait_ge(sem("top_ready"), t + 1)
                act.activation(prob[:, t, :], top[:, t, 0:TOPK], ACT.Exp, bias=ntop[:, t:t + 1],
                               accum_out=psum_[:, t:t + 1]).then_inc(sem("prob_ready"), 1)
            act.wait_ge(sem("gate_ready"), 1)
            dma(normf[:], A["norm_f_g"].rearrange("(o d) -> o d", o=1).to_broadcast([P, D]), "normf_in")
            for c in range(1, PASSES):
                act.copy(table[:, T:2 * T, c * E:(c + 1) * E], table[:, T:2 * T, 0:E]).then_inc(sem("gates_ready"), 1)

            def pair_steps(n, i, pair):
                p = n * 2 + i
                act.wait_ge(sem("gt_ready"), p * 2 + 2)
                act.wait_ge(sem("gated"), AHEAD + p)
                act.activation(sg, gt, ACT.Sigmoid, scale=ALPHA).then_inc(sem("sg_ready"), 1)
                act.wait_ge(sem("combined"), AHEAD + p * 4)
                act.wait_ge(sem("gtT_done"), p + 1)
                act.copy(gtT, bank[0][:, 0:T * P]).then_inc(sem("gtT_ready"), 1)
                for h in range(2):
                    act.wait_ge(sem("actT_done"), p * 2 + h + 1)
                    act.copy(actT[:, 4 * h:4 * h + 4, :], bank[h][:].rearrange("p (c s) -> p c s", c=4)).then_inc(sem("actT_ready"), 1)
                act.wait_ge(sem("half_done"), p * 3 + 3)
                act.copy(yy[:, 0:HALF], bank[4][:]).then_inc(sem("y0_ready"), 1)

            with act.Fori(0, BODIES) as n:
                for i in range(2):
                    pair_steps(n, i, n * 2 + i)
            over = overflowed(act)
            with act.If(over > 0):
                with act.Fori(1, PASSES) as c:
                    with act.Fori(0, BODIES) as n:
                        for i in range(2):
                            pair_steps(c * BODIES + n, i, n * 2 + i)
                act.wait_ge(sem("added"), AHEAD + PASSES * PAIRS * 4)
            for q in range(T * NH):
                act.wait_ge(sem("added"), AHEAD + PAIRS * 4 - T * NH + q + 1)
                t, r = q % T, slice(q // T * HALF, (q // T + 1) * HALF)
                act.activation((gt, sg)[t][:, r], x[:, t, r], ACT.Square,
                               accum_out=ssc[:, NH * t + q // T:NH * t + q // T + 1]).then_inc(sem("normf_sum"), 1)

        @block.tensor
        def _(pe):
            def mm(o, l, r, first, last):
                return pe.matmul(o, l, r, start=first, stop=last)

            def turn(rows, t, h, b0, name):
                for c in range(4):
                    ins = pe.transpose(bank[b0 + 2 * t + h][:, c * P:(c + 1) * P],
                                       rows[:, t, (4 * h + c) * P:(4 * h + c + 1) * P], ident)
                    if c == 2 and b0 == 0 and t == 0 and h == 0:
                        ins.then_inc(ring_read, AHEAD)
                ins.then_inc(sem(name), 1)

            def keep_clock(n, b):
                for _ in range(n):
                    mm(bank[b][:, 0:P], zeros, zeros, True, True)

            pe.wait_ge(sem("zeros_set"), 1)
            keep_clock(12, 7)
            pe.wait_ge(sem("ident_in"), 16)
            for t in range(T):
                pe.wait_ge(sem("hn_ready"), t + 1)
                for h in range(2):
                    turn(hn, t, h, 0, "hT_done")

            def columns_first(s, b0, name, between=None):
                w = front_block(s)
                if s:
                    pe.wait_ge(sem(f"front_in{s}"), 16)
                for m in range(HEADS):
                    if s == 0 and m % 2 == 0:
                        pe.wait_ge(sem(f"front_in0_{m // 2}"), 16)
                    if m == 2 and between:
                        between()
                    for c in range(KC):
                        if s == 0 and m == 0 and c % 4 == 0:
                            pe.wait_ge(sem("hT_ready"), 3 + c // 4)
                        if c == KC - 1 and m == HEADS - 1:
                            ins.then_inc(ring_read, 1)
                        ins = mm(bank[b0 + m // 2][:, m % 2 * SEQ:(m % 2 + 1) * SEQ], w[:, c, m * P:(m + 1) * P],
                                 hT[:, c, :], c == 0, c == KC - 1)
                    if m % 2:
                        ins.then_inc(ring_read if m == HEADS - 1 else sem(name), 1)

            def tokens_first(s, name):
                w = front_block(s)
                pe.wait_ge(sem(f"front_in{s}"), 16)
                for t in range(T):
                    for c in range(KC):
                        if c == KC - 1 and t == T - 1:
                            ins.then_inc(ring_read, 1)
                        ins = mm(bank[t][:], hT[:, c, t * P:(t + 1) * P], w[:, c, :], c == 0, c == KC - 1)
                    ins.then_inc(ring_read if t == T - 1 else sem(name), 1)

            def score(n):
                half = LEVELS[n] if n < len(LEVELS) else 0
                if half:
                    pe.wait_ge(sem("level_ready"), n + 1)
                    m = lv[n % 4].rearrange("p (h t) -> p h t", h=HEADS)
                    keys, queries = m, m
                else:
                    keys, queries = (b.rearrange("p (h t) -> p h t", h=HEADS) for b in (ks, qs))
                for h in range(HEADS):
                    if half == 128:
                        ins = mm(bank[4][:, h * P:(h + 1) * P], keys[:, h, 0:P], queries[:, h, P:2 * P], True, True)
                        continue
                    for t in range(T):
                        a = h * T + t
                        if half == 64:
                            ins = mm(bank[5][0:64, a * 64:(a + 1) * 64], keys[:, h, t * P:t * P + 64],
                                     queries[:, h, t * P + 64:t * P + 128], True, True)
                        elif half == 32:
                            for b in range(2):
                                o = t * P + 64 * b
                                ins = mm(bank[6][64 * b:64 * b + 32, a * 32:(a + 1) * 32], keys[:, h, o:o + 32],
                                         queries[:, h, o + 32:o + 64], True, True)
                        else:
                            bk, c0 = {3: (7, 0), 4: (7, 256), 5: (4, 0), 6: (4, 256), 7: (5, 0), 8: (5, 256)}[n]
                            for b in range(4):
                                o = t * P + 32 * b
                                ins = mm(bank[bk][32 * b:32 * b + 32, c0 + a * 32:c0 + (a + 1) * 32],
                                         keys[:, h, o:o + 32], queries[:, h, o:o + 32], True, True)
                ins.then_inc(sem("scored"), 1)

            columns_first(0, 4, "f_done")
            columns_first(1, 6, "q_done")
            tokens_first(2, "v_done")
            for n in range(3):
                score(n)
            columns_first(3, 2, "u_done", lambda: score(3))
            score(4)
            pe.wait_ge(sem("coarse_ready"), 4)
            for n in range(5, 9):
                score(n)
            pe.wait_ge(sem("v_ready"), 2)
            tokens_first(4, "g_done")
            pe.wait_ge(sem("rest_in"), 96)
            pe.wait_ge(sem("consts_in"), 16)
            for g in range(HEADS):
                pe.wait_ge(sem("pool_in"), g + 1)
                pe.wait_ge(sem("u_ready"), 2)
                ins = mm(bank[2 + g // 2][:, g % 2 * SEQ:(g % 2 + 1) * SEQ], pool_w[:, g, :], uu[:, g, :], True, True)
                if g % 2:
                    ins.then_inc(sem("pool_done"), 1)
            pe.wait_ge(sem("diag_ready"), 4)
            for t in range(T):
                for h in range(HEADS):
                    o = bank[6 + t][:, h * P:(h + 1) * P]
                    v_h = [vv[:, u, h * P:(h + 1) * P] for u in range(T)]
                    ins = mm(o, scT[:, h * T + t, :], v_h[t], True, t == 0)
                    if t:
                        ins = mm(o, scX[:, h, :], v_h[0], False, True)
                ins.then_inc(sem("o_done"), 1)
            def w_out_rows(t, nh, s):
                rows, c0 = w_out_half(s), 4 if s == 5 else 0
                for c in range(4):
                    if t == T - 1 and nh == NH - 1 and c == 3:
                        ins.then_inc(ring_read, 1)
                    ins = mm(bank[2 * t + nh][:], ocT[:, c0 + c, t * P:(t + 1) * P],
                             rows[:, c, nh * HALF:(nh + 1) * HALF], s == 5 and c == 0, s == 6 and c == 3)
                return ins

            pe.wait_ge(sem("front_in5"), 16)
            pe.wait_ge(sem("gg_ready"), 2)
            for nh in range(NH):
                pe.wait_ge(sem("pooled_ready"), 4)
                w_out_rows(0, nh, 5)
            for t in range(T):
                pe.wait_ge(sem("o_ready"), t + 1)
                for h in range(HEADS):
                    ins = pe.transpose(bank[4 + h // 2][:, h % 2 * SEQ + t * P:h % 2 * SEQ + (t + 1) * P],
                                       ob[:, t, h * P:(h + 1) * P], ident)
                    if t and h % 2:
                        ins.then_inc(sem("oT_done"), 1)
            for nh in range(NH):
                ins = w_out_rows(1, nh, 5)
            ins.then_inc(ring_read, 1)
            pe.wait_ge(sem("front_in6"), 16)
            pe.wait_ge(sem("heads_ready"), HEADS)
            for nh in range(NH):
                w_out_rows(0, nh, 6).then_inc(sem("proj_done"), 1)
            w_out_rows(1, 0, 6).then_inc(sem("proj_done"), 1)

            def route(t, chunks=range(KC)):
                for c in chunks:
                    if c % 4 == 0:
                        pe.wait_ge(sem("hT2_ready"), 2 * t + c // 4 + 1)
                    ins = mm(bank[t][:, 0:E], hT[:, c, t * P:(t + 1) * P], router[:, c, :], c == 0, c == KC - 1)
                if chunks[-1] == KC - 1:
                    ins.then_inc(sem("logits_done"), 1)

            for q in range(3):
                pe.wait_ge(sem("mixed"), q + 1)
                turn(x, q // 2, q % 2, 4, "hT2_done")
            w_out_rows(1, 1, 6).then_inc(ring_read, 1)
            route(0, range(KC // 2))
            pe.wait_ge(sem("mixed"), 4)
            turn(x, 1, 1, 4, "hT2_done")
            route(0, range(KC // 2, KC))
            route(1)
            pe.wait_ge(sem("chosen_ready"), 1)
            mm(bank[2][:, 0:E], before, chosen[:, 0, :], True, True).then_inc(sem("pos_done"), 1)
            mm(bank[3][:, 0:E], ones, chosen[:, 0, :], True, False)
            pe.wait_ge(sem("chosen_ready"), 2)
            mm(bank[3][:, 0:E], before, chosen[:, 1, :], False, True).then_inc(sem("pos_done"), 1)

            def gather():
                for c in range(KC):
                    for t in range(T):
                        ins = mm(bank[6 + c // 4][:, c % 4 * P:(c % 4 + 1) * P], hn[:, t, c * P:(c + 1) * P],
                                 pick[:, t, :], t == 0, t == T - 1)
                    if c % 4 == 3:
                        ins.then_inc(sem("gathered"), 1)

            pe.wait_ge(sem("pick_ready"), 1)
            pe.wait_ge(sem("rows_ready"), 2)
            gather()
            mm(bank[2][:, 0:E], ones, chosen[:, 0, :], True, False)
            mm(bank[2][:, 0:E], ones, chosen[:, 1, :], False, True).then_inc(sem("count_done"), 1)

            def product(n, i, m, b0, lhs, operand, mid=None):
                for nh in range(NH):
                    mm(bank[b0 + nh][:], which[:, i, :], bias[0:E, m, nh * HALF:(nh + 1) * HALF], True, False)
                for k in range(QUARTERS):
                    j = 2 * QUARTERS * m + 2 * k
                    for e in range(2):
                        pe.wait_ge(landed[slot_of(i, j + e)], landed_at(n, i, j + e))
                    if k % 2 == 0:
                        operand(k // 2)
                    if k == 2 and mid:
                        mid()
                    for nh in range(NH):
                        for c in range(ROWS * k, ROWS * (k + 1)):
                            for e in range(2):
                                r = slice(e * SLOTS, (e + 1) * SLOTS)
                                ins = mm(bank[b0 + nh][r, :], lhs[:, c, r],
                                         ring[:, slot_of(i, j + e), c % ROWS, nh * HALF:(nh + 1) * HALF],
                                         False, c == KC - 1)
                                if c % ROWS == ROWS - 1 and nh == NH - 1:
                                    ins.then_inc(ring_read, 1)
                        if k == QUARTERS - 1 and nh == 0:
                            ins.then_inc(sem("half_done"), 1)

            def pair_steps(n, i, pair):
                p = n * 2 + i
                pe.wait_ge(sem("actT_ready"), AHEAD + p * 2)
                product(n, i, 0, 0, xsT[i], lambda h: pe.wait_ge(sem("xs_ready"), p * 2 + h + 1))

                def gates_turned():
                    pe.wait_ge(sem("gt_ready"), p * 2 + 2)
                    pe.wait_ge(sem("pickg_ready"), p + 1)
                    for t in range(T):
                        ins = pe.transpose(bank[0][:, t * P:(t + 1) * P], pickg[:, t, :], ident)
                    ins.then_inc(sem("gtT_done"), 1)

                pe.wait_ge(sem("up_read"), AHEAD + p * 2)
                product(n, i, 1, 2, xsT[i], lambda h: None, gates_turned)
                pe.wait_ge(sem("pick_ready"), p + 2)
                pe.wait_ge(sem("added"), AHEAD + p * 4)
                gather()
                pe.wait_ge(sem("gtT_ready"), p + 1)
                for h in range(2):
                    pe.wait_ge(sem("act_ready"), p * 2 + h + 1)
                    for c in range(4):
                        ins = pe.transpose(bank[h][:, c * P:(c + 1) * P],
                                           up[:, (4 * h + c) * P:(4 * h + c + 1) * P], ident)
                    ins.then_inc(sem("actT_done"), 1)
                product(n, i, 2, 4, actT, lambda h: pe.wait_ge(sem("actT_ready"), AHEAD + p * 2 + h + 1))
                pe.wait_ge(sem("xs_ready"), p * 2 + 4)
                for nh in range(NH):
                    pe.wait_ge(sem(f"y{nh}_ready"), p + 1)
                    for t in range(T):
                        mm(bank[6 - 2 * nh + t][:], gtT[:, t * P:(t + 1) * P], yy[:, nh * HALF:(nh + 1) * HALF],
                           True, True).then_inc(sem("combined"), 1)

            pe.wait_ge(sem("bias_in"), 48)
            with pe.Fori(0, BODIES) as n:
                for i in range(2):
                    pair_steps(n, i, n * 2 + i)
            over = overflowed(pe)
            with pe.If(over > 0):
                with pe.Fori(1, PASSES) as c:
                    with pe.Fori(0, BODIES) as n:
                        for i in range(2):
                            pair_steps(c * BODIES + n, i, n * 2 + i)

        @block.vector
        def _(dve):
            steps = [0]

            def seq(ins):
                steps[0] += 1
                ins.then_inc(sem("dve_step"), 1)
                dve.wait_ge(sem("dve_step"), steps[0])

            def ahead(ins, name):
                ins.then_inc(sem(name), AHEAD)
                dve.wait_ge(sem(name), AHEAD)

            def mean(o, i, scale, name):
                dve.tensor_scalar(o, i, scale, EPS, ALU.mult, ALU.add).then_inc(sem(name), 1)

            for t in range(T):
                dve.wait_ge(sem("norm1_sum"), t + 1)
                mean(ms[:, t:t + 1], ss[:, t:t + 1], 1.0 / D, "norm1_mean")
            for t in range(T):
                dve.wait_ge(sem("norm1_rstd"), t + 1)
                dve.tensor_scalar(hn[:, t, :], x[:, t, :], rstd[:, t:t + 1], None, ALU.mult).then_inc(sem("hn_ready"), 1)

            def from_turned(t, h, b0, g, done, name):
                dve.wait_ge(sem(done), 2 * t + h + 1)
                dve.tensor_tensor(hT[:, 4 * h:4 * h + 4, t * P:(t + 1) * P],
                                  bank[b0 + 2 * t + h][:].rearrange("p (c t) -> p c t", c=4),
                                  g[:, 4 * h:4 * h + 4].unsqueeze(2).broadcast_to([P, 4, P]),
                                  ALU.mult).then_inc(sem(name), 1)

            dve.wait_ge(sem("g1_in"), 16)
            for t in range(T):
                for h in range(2):
                    from_turned(t, h, 0, g1, "hT_done", "hT_ready")
            dve.wait_ge(sem("lb_in"), 32)
            dve.tensor_tensor(two[:], lbr[:, 0, :], lbr[:, 1, :], ALU.subtract).then_inc(sem("lb_diff"), 1)
            dve.wait_ge(sem("lb_ready"), 1)
            seq(dve.tensor_scalar(oml[:], lb[:], -1.0, 1.0, ALU.mult, ALU.add))
            for h in range(HEADS):
                dve.wait_ge(sem("f_sig"), h // 2 + 1)
                ins = dve.tensor_scalar(fs[:, h * SEQ:(h + 1) * SEQ], fs[:, h * SEQ:(h + 1) * SEQ], oml[:, h:h + 1],
                                        lb[:, h:h + 1], ALU.mult, ALU.add)
                seq(ins)
            dve.tensor_scalar(ks, fs, -1.0, 1.0, ALU.mult, ALU.add).then_inc(sem("k_ready"), 1)
            dve.wait_ge(sem("resets"), 2)
            dve.wait_ge(sem("logf_ready"), 1)
            seq(dve.tensor_tensor_scan(bs, lv[3], fs, 0.0, ALU.mult, ALU.add))
            for b in range(2):
                dve.wait_ge(sem("q_sig"), b + 1)
                r = slice(b * HALF, (b + 1) * HALF)
                seq(dve.tensor_tensor(qs[:, r], bank[6 + b][:], lv[0][:, r], ALU.mult))

            kv, qv = ks, qs
            b4 = bs.rearrange("p (h c t) -> p h c t", h=HEADS, c=4)
            k4 = ks.rearrange("p (h c t) -> p h c t", h=HEADS, c=4)
            seq(dve.tensor_tensor(two[:], b4[:, :, 0, CHUNK - 1], b4[:, :, 1, CHUNK - 1], ALU.add))

            def wide(a):
                return a.broadcast_to([P, HEADS, CHUNK])

            for n, half in enumerate(LEVELS):
                m = lv[n % 4]
                m4 = m.rearrange("p (h c t) -> p h c t", h=HEADS, c=4)
                if n >= 4:
                    dve.wait_ge(sem("scored"), n - 3)
                if half == 128:
                    dve.tensor_tensor(m4[:, :, 0, :], wide(two[:].unsqueeze(2)), b4[:, :, 0, :], ALU.subtract)
                    dve.tensor_tensor(m4[:, :, 1, :], wide(b4[:, :, 1, CHUNK - 1:]), b4[:, :, 1, :], ALU.subtract)
                    dve.tensor_copy(m4[:, :, 2, :], b4[:, :, 2, :])
                    last = dve.tensor_tensor(m4[:, :, 3, :], b4[:, :, 3, :], wide(b4[:, :, 2, CHUNK - 1:]), ALU.add)
                elif half == 64:
                    for c in (0, 2):
                        dve.tensor_tensor(m4[:, :, c, :], wide(b4[:, :, c, CHUNK - 1:]), b4[:, :, c, :], ALU.subtract)
                        last = dve.tensor_copy(m4[:, :, c + 1, :], b4[:, :, c + 1, :])
                else:
                    bl, ml = lvl(bs, half), lvl(m, half)
                    blocks = HEADS * SEQ // (2 * half)
                    ref = bl[:, :, 0, half - 1:].broadcast_to([P, blocks, half])
                    dve.tensor_tensor(ml[:, :, 0, :], ref, bl[:, :, 0, :], ALU.subtract)
                    last = dve.tensor_tensor(ml[:, :, 1, :], bl[:, :, 1, :], ref, ALU.subtract)
                last.then_inc(sem("diff_ready"), 1)

                def finish(n):
                    half = LEVELS[n]
                    dve.wait_ge(sem("decay_ready"), n + 1)
                    ml, kl, ql = lvl(lv[n % 4], half), lvl(ks, half), lvl(qs, half)
                    dve.tensor_tensor(ml[:, :, 0, :], ml[:, :, 0, :], kl[:, :, 0, :], ALU.mult)
                    dve.tensor_tensor(ml[:, :, 1, :], ml[:, :, 1, :], ql[:, :, 1, :], ALU.mult).then_inc(sem("level_ready"), 1)

                if n:
                    finish(n - 1)
            finish(len(LEVELS) - 1)

            dve.wait_ge(sem("consts_in"), 16)
            seq(dve.memset(fs[:, 0:SEQ], 1.0))
            for g in range(HEADS):
                dve.wait_ge(sem("u_ready"), g // 2 + 1)
                ins = dve.tensor_tensor_scan(cs[:, g, :], fs[:, 0:SEQ], uu[:, g, :], 0.0, ALU.mult, ALU.add)
            seq(ins)
            for g, w in enumerate(WINDOWS):
                ins = dve.scalar_tensor_tensor(uu[:, g, w:], cs[:, g, 0:SEQ - w], 1.0 / w, uu[:, g, w:], ALU.mult, ALU.add)
            seq(ins)
            seq(dve.tensor_tensor(cs[:, :, 0:short.shape[2]], cs[:, :, 0:short.shape[2]], short, ALU.mult))
            for g, w in enumerate(WINDOWS):
                dve.scalar_tensor_tensor(uu[:, g, :], cs[:, g, :], 1.0 / w, uu[:, g, :], ALU.mult,
                                         ALU.subtract).then_inc(sem("pool_in"), 1)
            dve.wait_ge(sem("scored"), 9)
            for l, (bk, c0) in enumerate(((7, 0), (7, 256), (4, 0), (4, 256), (5, 0), (5, 256))):
                ins = dve.tensor_tensor(picked[:, l, :].rearrange("p (a t) -> p a t", a=8),
                                        bank[bk][:, c0:c0 + 256].rearrange("p (a t) -> p a t", a=8),
                                        masks[:, l, :].unsqueeze(1).broadcast_to([P, 8, SMALL]), ALU.mult)
            seq(ins)
            fine = lv[0][:, 0:256]
            seq(dve.tensor_reduce(fine, picked.rearrange("p l x -> p x l"), AX.X, ALU.add))
            for b in range(4):
                r = slice(32 * b, 32 * b + 32)
                dve.tensor_copy(scT[r, :, r], fine[r, :].rearrange("p (a t) -> p a t", a=8)).then_inc(sem("diag_ready"), 1)
            for t in range(T):
                dve.wait_ge(sem("g_sig"), t + 1)
                dve.tensor_tensor(gg[:, t, :], bank[t][:], sigg[:, t, :], ALU.mult).then_inc(sem("gg_ready"), 1)
            for t in range(T):
                dve.wait_ge(sem("o_squares"), t + 1)
                seq(dve.tensor_reduce(ss[:, 4 * t:4 * t + 4], osq[:, t, :].rearrange("p (h v) -> p h v", h=HEADS), AX.X, ALU.add))
                mean(ms[:, 4 * t:4 * t + 4], ss[:, 4 * t:4 * t + 4], 1.0 / P, "head_mean")
            dve.wait_ge(sem("gg_ready"), 2)
            for t in range(T):
                dve.wait_ge(sem("head_rstd"), t + 1)
                o3 = ob[:, t, :].rearrange("p (h v) -> p h v", h=HEADS)
                seq(dve.tensor_tensor(o3, bank[6 + t][:].rearrange("p (h v) -> p h v", h=HEADS),
                                      rstd[:, 4 * t:4 * t + 4].unsqueeze(2).broadcast_to([P, HEADS, P]), ALU.mult))
                dve.tensor_tensor(ob[:, t, :], ob[:, t, :], gg[:, t, :], ALU.mult).then_inc(sem("o_ready"), 1)
            def add_mixed(t, nh):
                r = slice(nh * HALF, (nh + 1) * HALF)
                if t and nh:
                    dve.wait_ge(ring_read, AHEAD + FRONT)
                else:
                    dve.wait_ge(sem("proj_done"), 2 * t + nh + 1)
                dve.tensor_tensor(x[:, t, r], bank[2 * t + nh][:], x[:, t, r], ALU.add).then_inc(sem("mixed"), 1)

            def mean_of_halves(o, i, t, name, sums):
                dve.wait_ge(sem(f"{name}_sum"), sums)
                seq(dve.tensor_tensor(i[:, 2 * t:2 * t + 1], i[:, 2 * t:2 * t + 1], i[:, 2 * t + 1:2 * t + 2], ALU.add))
                mean(o[:, t:t + 1], i[:, 2 * t:2 * t + 1], 1.0 / D, f"{name}_mean")

            def choose_experts(t):
                dve.wait_ge(sem("logits_done"), t + 1)
                dve.wait_ge(sem("norm2_rstd"), t + 1)
                seq(dve.scalar_tensor_tensor(logits[:, t, :], bank[t][:, 0:E], rstdb[:, t:t + 1], rbias[:],
                                             ALU.mult, ALU.add))
                seq(dve.max(top[:, t, :], logits[:, t, :]))
                seq(dve.max_index(topi[:, t, :], top[:, t, :], logits[:, t, :]))
                seq(dve.tensor_copy(topf[:, t * TOPK:(t + 1) * TOPK], topi[:, t, 0:TOPK]))
                h = hit[:, t * TOPK:(t + 1) * TOPK, :]
                seq(dve.tensor_tensor(h, expert_no.unsqueeze(1).broadcast_to([P, TOPK, E]),
                                      topf[:, t * TOPK:(t + 1) * TOPK].unsqueeze(2).broadcast_to([P, TOPK, E]),
                                      ALU.is_equal))
                dve.tensor_reduce(chosen[:, t, :], h.rearrange("p k e -> p e k"), AX.X, ALU.add).then_inc(sem("chosen_ready"), 1)
                dve.tensor_scalar(ntop[:, t:t + 1], top[:, t, 0:1], -1.0, None, ALU.mult).then_inc(sem("top_ready"), 1)

            def place_tokens(t):
                dve.wait_ge(sem("pos_done"), t + 1)
                dve.wait_ge(sem("chosen_ready"), t + 1)
                seq(dve.scalar_tensor_tensor(posn[:, t, :], bank[2 + t][:, 0:E], 1.0, chosen[:, t, :], ALU.add, ALU.mult))
                seq(dve.tensor_scalar(table[:, t, 0:E], posn[:, t, :], -1.0, None, ALU.add))
                return pick_slots(t, table[:, t, 0:2])

            def pick_slots(t, pos):
                return dve.tensor_tensor(pick[:, t, :].rearrange("p (e s) -> p e s", e=2),
                                         slot_no.unsqueeze(1).broadcast_to([P, 2, SLOTS]),
                                         pos.unsqueeze(2).broadcast_to([P, 2, SLOTS]), ALU.is_equal)

            def pick_rows(i, first):
                return dve.tensor_copy(which[:, i, :].rearrange("q (e s) -> q e s", e=2),
                                       ident[0:E, bass.ds(first, 2)].unsqueeze(2).broadcast_to([E, 2, SLOTS]))

            def pick_gates(pos, gates):
                for t in range(T):
                    for e in range(2):
                        b = dve.tensor_scalar(pickg[:, t, e * SLOTS:(e + 1) * SLOTS], slot_no, pos[:, t, e:e + 1],
                                              gates[:, t, e:e + 1], ALU.is_equal, ALU.mult)
                b.then_inc(sem("pickg_ready"), 1)

            dve.wait_ge(sem("rest_in"), 96)
            dve.wait_ge(sem("table_set"), 1)
            for nh in range(NH):
                add_mixed(0, nh)
            mean_of_halves(msb, ssb, 0, "norm2", NH)
            add_mixed(1, 0)
            for h in range(2):
                from_turned(0, h, 4, g2, "hT2_done", "hT2_ready")
            add_mixed(1, 1)
            from_turned(1, 0, 4, g2, "hT2_done", "hT2_ready")
            mean_of_halves(msb, ssb, 1, "norm2", 2 * NH)
            from_turned(1, 1, 4, g2, "hT2_done", "hT2_ready")
            choose_experts(0)
            choose_experts(1)
            pick_rows(0, 0)
            seq(place_tokens(0))
            place_tokens(1).then_inc(sem("pick_ready"), 1)
            dve.wait_ge(sem("prob_ready"), 2)
            ahead(dve.reciprocal(rps[:], psum_[:]), "actT_ready")
            ahead(dve.tensor_tensor(prob[:], prob[:], rps[:].unsqueeze(2).broadcast_to([P, T, TOPK]), ALU.mult), "gated")
            ahead(dve.tensor_tensor(hitg[:], hit[:],
                                    prob[:].rearrange("p t k -> p (t k)").unsqueeze(2).broadcast_to([P, T * TOPK, E]),
                                    ALU.mult), "combined")
            dve.tensor_reduce(table[:, T:2 * T, 0:E], hitg[:].rearrange("p (t k) e -> p t e k", t=T), AX.X,
                              ALU.add).then_inc(sem("gate_ready"), 1)

            def choose(p, i, pair):
                dve.tensor_copy(cur[:], table[:, :, bass.ds(p * 2 + 2, 2)]).then_inc(sem("cur_ready"), 1)
                dve.wait_ge(sem("cur_ready"), p + 1)
                pick_rows(1 - i, dve.snap((pair + 1) % PAIRS * 2))
                for t in range(T):
                    a = pick_slots(t, cur[:, t, :])
                a.then_inc(sem("pick_ready"), 1)
                pick_gates(cur[:, 0:T, :], cur[:, T:2 * T, :])

            def gathered_rows(buf, count):
                for h in range(2):
                    dve.wait_ge(sem("gathered"), count + h + 1)
                    dve.tensor_tensor(buf[:, 4 * h:4 * h + 4, :], bank[6 + h][:].rearrange("p (c s) -> p c s", c=4),
                                      g2[:, 4 * h:4 * h + 4].unsqueeze(2).broadcast_to([P, 4, P]),
                                      ALU.mult).then_inc(sem("xs_ready"), 1)

            gathered_rows(xsT[0], 0)
            dve.wait_ge(sem("gate_ready"), 1)
            pick_gates(table[:, 0:T, 0:2], table[:, T:2 * T, 0:2])
            for c in range(1, PASSES):
                ins = dve.tensor_scalar(table[:, 0:T, c * E:(c + 1) * E], posn[:], -1.0 - c * SLOTS, None, ALU.add)
            ahead(ins, "added")
            dve.wait_ge(sem("gates_ready"), PASSES - 1)
            dve.wait_ge(sem("count_done"), 1)
            ahead(dve.tensor_reduce(most[:], bank[2][:, 0:E], AX.X, ALU.max), "up_read")
            dve.tensor_scalar(flag[:], most[:], float(SLOTS), None, ALU.is_gt).then_inc(sem("flag_ready"), 1)

            def pair_steps(n, i, pair):
                p = n * 2 + i
                first = AHEAD + p * CPP + FRONT
                for h in range(2):
                    if h:
                        dve.wait_ge(ring_read, first + CPP // 3)
                    else:
                        dve.wait_ge(sem("half_done"), p * 3 + 1)
                    dve.tensor_scalar(gt[:, h * HALF:(h + 1) * HALF], bank[h][:], LIMIT, None, ALU.min)\
                       .then_inc(sem("gt_ready"), 1)
                dve.wait_ge(sem("sg_ready"), p + 1)
                dve.tensor_tensor(gt, gt, sg, ALU.mult).then_inc(sem("gated"), 1)
                dve.wait_ge(sem("gtT_done"), p + 1)
                dve.wait_ge(sem("gathered"), p * 2 + 2)
                choose(p, i, pair)
                for h in range(2):
                    if h:
                        dve.wait_ge(ring_read, first + 2 * CPP // 3)
                    else:
                        dve.wait_ge(sem("half_done"), p * 3 + 2)
                    dve.tensor_scalar(up[:, h * HALF:(h + 1) * HALF], bank[2 + h][:], LIMIT, -LIMIT, ALU.min,
                                      ALU.max).then_inc(sem("up_read"), 1)
                dve.wait_ge(sem("gated"), AHEAD + p + 1)
                for h in range(2):
                    dve.wait_ge(sem("up_read"), AHEAD + p * 2 + h + 1)
                    r = slice(h * HALF, (h + 1) * HALF)
                    dve.scalar_tensor_tensor(up[:, r], up[:, r], 1.0, gt[:, r], ALU.add, ALU.mult).then_inc(sem("act_ready"), 1)
                gathered_rows(xsT[1 - i], p * 2 + 2)
                dve.wait_ge(ring_read, first + CPP)
                dve.wait_ge(sem("combined"), AHEAD + p * 4)
                dve.tensor_copy(yy[:, HALF:D], bank[5][:]).then_inc(sem("y1_ready"), 1)
                dve.wait_ge(sem("added"), AHEAD + p * 4)
                for nh in range(NH):
                    for t in range(T):
                        r = slice(nh * HALF, (nh + 1) * HALF)
                        dve.wait_ge(sem("combined"), AHEAD + p * 4 + T * nh + t + 1)
                        dve.tensor_tensor(x[:, t, r], bank[6 - 2 * nh + t][:], x[:, t, r], ALU.add).then_inc(sem("added"), 1)

            with dve.Fori(0, BODIES) as n:
                for i in range(2):
                    pair_steps(n, i, n * 2 + i)
            over = overflowed(dve)
            with dve.If(over > 0):
                with dve.Fori(1, PASSES) as c:
                    with dve.Fori(0, BODIES) as n:
                        for i in range(2):
                            pair_steps(c * BODIES + n, i, n * 2 + i)
                dve.wait_ge(sem("added"), AHEAD + PASSES * PAIRS * 4)
            dve.wait_ge(sem("added"), AHEAD + PAIRS * 4)
            dve.wait_ge(sem("normf_in"), 16)
            for t in range(T):
                mean_of_halves(msc, ssc, t, "normf", T * (NH - 1) + t + 1)
            for t in range(T):
                dve.wait_ge(sem("normf_rstd"), t + 1)
                for nh in range(NH):
                    r = slice(nh * HALF, (nh + 1) * HALF)
                    dve.scalar_tensor_tensor(x[:, t, r], x[:, t, r], rstdc[:, t:t + 1], normf[:, r], ALU.mult,
                                             ALU.mult).then_inc(sem("out_ready"), 1)


_INS = ["x", "norm1_g", "w_in", "hgrn_lb", "hgrn_norm_g", "pool_w", "pool_scale", "w_out", "norm2_g", "router_w",
        "router_b", "w_gate", "b_gate", "w_up", "b_up", "w_down", "b_down", "norm_f_g"]


def kernel(**inputs):
    import concourse.bacc as _bacc
    from concourse.bass_utils import run_bass_kernel_spmd as _run

    nc = _bacc.Bacc("TRN2", target_bir_lowering=False, num_devices=1)
    arrays, args = {}, {}
    for name in _INS:
        arrays[f"in_{name}"] = np.ascontiguousarray(inputs[name])
    arrays["in_consts"] = layer_constants()[0]
    for name, a in arrays.items():
        args[name[3:]] = nc.dram_tensor(name, a.shape, mybir.dt.from_np(a.dtype), kind="ExternalInput").ap()
    out = nc.dram_tensor("out", (1, SEQ, D), F32, kind="ExternalOutput").ap()
    hybrid_hgrn2_pool_moe(nc, args, out)
    r = _run(nc, [arrays], core_ids=[0])
    return r.results[0]["out"]
```

```python
from contextlib import ExitStack

import numpy as np

import concourse.bass as bass
from concourse import mybir

ALU = mybir.AluOpType
ACT = mybir.ActivationFunctionType
AX = mybir.AxisListType
F32 = mybir.dt.float32
I32 = mybir.dt.int32
U32 = mybir.dt.uint32

P = 128
D = 1024
SEQ = 256
T = SEQ // P
KC = D // P
HALF = 512
NH = D // HALF
HEADS = 4
CHUNK = 64
LEVELS = (128, 64, 32, 16, 8, 4, 2, 1)
SMALL = 32
WINDOWS = (2, 4, 8, 16)
E = 32
TOPK = 4
SLOTS = 64
PASSES = SEQ // SLOTS
PAIRS = E // 2
BODIES = PAIRS // 2
ROWS = 2
RING = 16
QUARTERS = KC // ROWS
CPP = 3 * QUARTERS * 2
FRONT = 14
AHEAD = 1
LIMIT = 7.0
ALPHA = 1.702
EPS = 1e-6
WORK = 12 * D + 3 * T * P
TAB = PASSES * E + 2


def layer_constants():
    t = np.arange(P)
    parts = {
        "ident": np.eye(P),
        "before": (t[:, None] < t[None, :]) * 1.0,
        "ones": np.ones((P, P)),
        "slot": np.tile(np.arange(SLOTS), (P, 1)),
        "expert": np.tile(np.arange(E), (P, 1)),
    }
    s, u = t[:, None] % SMALL, np.arange(SMALL)[None, :]
    masks = [(s // h % 2 == 0) & (u // h == s // h + 1) for h in LEVELS if h < SMALL] + [s == u]
    parts["masks"] = np.concatenate(masks, 1)
    w = max(WINDOWS)
    parts["thrice"] = (t[:, None] % E == np.arange(E)[None, :]) * 1.0
    parts["short"] = np.tile(np.concatenate([n / np.minimum(np.arange(1, w + 1), n) for n in WINDOWS]), (P, 1))
    at, cols = {}, 0
    for k, a in parts.items():
        at[k] = (cols, a.shape[1])
        cols += a.shape[1]
    return np.concatenate([a.astype(np.float32) for a in parts.values()], 1), at


def hybrid_hgrn2_pool_moe(nc, A, out):
    _, const_at = layer_constants()
    w_in = A["w_in"][0].rearrange("(c p) n -> p c n", p=P)
    w_out = A["w_out"][0].rearrange("(c p) n -> p c n", p=P)
    x_dram = A["x"][0].rearrange("(t p) d -> p t d", p=P)
    out_dram = out[0].rearrange("(t p) d -> p t d", p=P)

    with ExitStack() as ctx:
        sems = {}

        def sem(name):
            if name not in sems:
                sems[name] = ctx.enter_context(nc.semaphore(name))
            return sems[name]

        def sb(name, shape, dt=F32):
            return ctx.enter_context(nc.sbuf_tensor(name, shape, dt))

        bank = [ctx.enter_context(nc.psum_tensor(f"bank{i}", [P, HALF], F32)) for i in range(8)]

        ring = sb("ring", [P, RING, ROWS, D])
        x = sb("x", [P, T, D])
        hn = sb("hn", [P, T, D])
        consts = sb("consts", [P, sum(n for _, n in const_at.values())])
        work = sb("work", [P, WORK])
        which = sb("which", [3 * E, 2, P])[:]

        at = [0]

        def view(n):
            at[0] += n
            return work[:, at[0] - n:at[0]]

        hT = view(KC * SEQ).rearrange("p (c t) -> p c t", c=KC)
        vv = view(T * HALF).rearrange("p (t n) -> p t n", t=T)
        scT = view(HEADS * T * P).rearrange("p (a t) -> p a t", t=P)
        scX = view(HEADS * P).rearrange("p (h t) -> p h t", t=P)
        fs = view(HEADS * SEQ)
        picked = work[:, at[0]:at[0] + 6 * SEQ].rearrange("p (l x) -> p l x", l=6)
        ks = view(HEADS * SEQ)
        bs = view(HEADS * SEQ)
        qs = view(HEADS * SEQ)
        lv = [view(HEADS * SEQ) for _ in range(4)]
        gg = fs.rearrange("p (t n) -> p t n", t=T)
        ob = qs.rearrange("p (t n) -> p t n", t=T)
        osq = lv[0].rearrange("p (t n) -> p t n", t=T)
        sigg = lv[1].rearrange("p (t n) -> p t n", t=T)
        ocT = work[:, at[0] - 2 * HEADS * SEQ:at[0]].rearrange("p (c t) -> p c t", c=KC)
        uu = hn[:, 0, :].rearrange("p (g t) -> p g t", g=HEADS)
        cs = hn[:, 1, :].rearrange("p (g t) -> p g t", g=HEADS)
        at[0] = 0
        xsT = [view(KC * P).rearrange("p (c s) -> p c s", c=KC) for _ in range(2)]
        bias = view(D)
        spare = [view(D) for _ in range(3)]
        parts = spare[2][:, 0:T * P].rearrange("p (t s) -> p t s", t=T)
        gt, sg, up, yy = (view(D) for _ in range(4))
        spare.append(view(D))
        actT = view(D).rearrange("p (c s) -> p c s", c=KC)
        gtT = view(T * P)
        pick = view(T * P).rearrange("p (t s) -> p t s", t=T)
        pickg = view(T * P).rearrange("p (t s) -> p t s", t=T)
        assert at[0] <= WORK

        def small(name, n, dt=F32):
            return sb(name, [P, n], dt)

        g1, g2 = small("g1", KC), small("g2", KC)
        lbr = sb("lbr", [P, 2, HEADS])
        lb, oml = small("lb", HEADS), small("oml", HEADS)
        pool_w = sb("pool_w_sb", [P, HEADS, P])
        pool_s, hnorm = small("pool_s", HEADS), small("hnorm", 1)
        router = sb("router", [P, KC, E])
        rbias = small("rbias", E)
        ss, ms, rstd, expo = small("ss", 8), small("ms", 8), small("rstd", 8), small("expo", 8)
        expo2 = small("expo2", 8)
        ssb, rstdb, rstdc = small("ssb", 4), small("rstdb", 2), small("rstdc", 2)
        ssc, msb, msc = small("ssc", 4), small("msb", 2), small("msc", 2)
        two = small("two", HEADS)
        logits = sb("logits", [P, T, E])
        top = sb("top", [P, T, 8])
        topi = sb("topi", [P, T, 8], U32)
        ntop, psum_, rps = small("ntop", T), small("psum_", T), small("rps", T)
        prob = sb("prob", [P, T, TOPK])
        hit = sb("hit", [P, T * TOPK, E])
        hitg = sb("hitg", [P, T * TOPK, E])
        chosen = sb("chosen", [P, T, E])
        posn = sb("posn", [P, T, E])
        table = sb("table", [P, 2 * T, TAB])
        cur = sb("cur", [P, 2 * T, 2])
        most = small("most", 1)
        flag = sb("flag", [P, 1], I32)

        def const(name):
            a, n = const_at[name]
            return consts[:, a:a + n]

        ident, before, ones, thrice = const("ident"), const("before"), const("ones"), const("thrice")
        slot_no, expert_no = const("slot"), const("expert")
        masks = const("masks").rearrange("p (l t) -> p l t", t=SMALL)
        short = const("short").rearrange("p (g t) -> p g t", g=len(WINDOWS))

        landed = [sem(f"landed{s}") for s in range(RING)]
        ring_read = sem("ring_read")

        def slot_of(i, j):
            return (FRONT + CPP * i + j) % RING

        def row_by_row(q):
            return q >= 2 * CPP - 2

        def landed_at(n, i, j):
            turns = (FRONT + CPP * i + j) // RING + (slot_of(i, j) >= FRONT)
            return 16 * turns + n * (16 * 2 * CPP // RING)

        back = FRONT - RING + 1

        aside = ((19, (gt, sg)), (21, (up, yy)),
                 (26, (actT.rearrange("p c s -> p (c s)"), xsT[1].rearrange("p c s -> p (c s)"))),
                 (33, (spare[0], spare[1])), (40, (spare[2], spare[3])))

        def chunk(experts, j):
            w = A[("w_gate", "w_up", "w_down")[j // (2 * QUARTERS)]]
            c = ROWS * (j % (2 * QUARTERS) // 2)
            return w[0, experts[j % 2]].rearrange("(c p) n -> p c n", p=P)[:, c:c + ROWS, :]

        def load_aside(eng, k):
            q, rows = aside[k]
            for c in range(ROWS):
                src = chunk((q // CPP * 2, q // CPP * 2 + 1), q % CPP)[:, c, :]
                eng.dma_start(rows[c], src).then_inc(sem(f"aside_in{k}"), 16)

        def from_aside(eng, k):
            j, rows = aside[k]
            eng.wait_ge(sem(f"aside_in{k}"), 16 * ROWS)
            eng.wait_ge(ring_read, AHEAD + j + back)
            for c in range(ROWS):
                ins = eng.tensor_copy(ring[:, slot_of(0, j), c], rows[c])
            ins.then_inc(landed[slot_of(0, j)], 16)

        def aside_used(eng, k):
            j = aside[k][0]
            eng.wait_ge(landed[slot_of(0, j)], landed_at(0, 0, j))

        def w_out_half(s):
            return ring[:, 2 * s:2 * s + 2].rearrange("p s c n -> p (s c) n")

        def front_block(s):
            return ring[:, 2 * s:2 * s + 2].rearrange("p s c n -> p (s c n)").rearrange("p (c n) -> p c n", c=KC)

        def overflowed(eng):
            eng.wait_ge(sem("flag_ready"), 1)
            return eng.value_load(flag[0:1, 0:1], min_val=0, max_val=1)

        def product_done(eng, name, b, s):
            if b == 0:
                eng.wait_ge(sem(name), 1)
            else:
                eng.wait_ge(ring_read, AHEAD + 2 * s + 2)

        def lvl(b, half):
            return b.rearrange("p (n two h) -> p n two h", two=2, h=half)

        block = ctx.enter_context(nc.Block())

        @block.sync
        def _(sp):
            for t in range(T):
                sp.dma_start(x[:, t, :], x_dram[:, t, :]).then_inc(sem(f"x_in{t}"), 16)
            for s, col in enumerate((1, 0, 2, 4, 3)):
                if s:
                    sp.dma_start(front_block(s), w_in[:, :, col * HALF:(col + 1) * HALF]).then_inc(sem(f"front_in{s}"), 16)
                    continue
                for h in range(2):
                    r = slice(h * HALF // 2, (h + 1) * HALF // 2)
                    sp.dma_start(front_block(s)[:, :, r],
                                 w_in[:, :, col * HALF:(col + 1) * HALF][:, :, r]).then_inc(sem(f"front_in0_{h}"), 16)
            for s, h in ((5, 1), (6, 0)):
                sp.dma_start(w_out_half(s), w_out[:, 4 * h:4 * h + 4, :]).then_inc(sem(f"front_in{s}"), 16)

            def load(i, j, experts):
                slot = slot_of(i, j)
                if not row_by_row(CPP * i + j):
                    sp.dma_start(ring[:, slot], chunk(experts, j)).then_inc(landed[slot], 16)
                    return
                sp.dma_start(ring[:, slot, 0], chunk(experts, j)[:, 0, :]).then_inc(landed[slot], 16)
                if j == CPP - 1:
                    for e in range(2):
                        sp.dma_start(ring[:, slot_of(i, j - 1 + e), 1],
                                     chunk(experts, j - 1 + e)[:, 1, :]).then_inc(sem(f"last_row{e}"), 16)

            for q in range(2 * CPP):
                if q not in [k for k, _ in aside]:
                    if q + back > 0:
                        sp.wait_ge(ring_read, AHEAD + q + back)
                    load(q // CPP, q % CPP, (q // CPP * 2, q // CPP * 2 + 1))

            def load_pair(n, i, pair):
                p = n * 2 + i
                experts = [sp.snap(pair * 2), sp.snap(pair * 2 + 1)]
                for j in range(CPP):
                    sp.wait_ge(ring_read, AHEAD + p * CPP + j + back)
                    load(i, j, experts)

            with sp.Fori(1, BODIES) as n:
                for i in range(2):
                    load_pair(n, i, n * 2 + i)
            over = overflowed(sp)
            with sp.If(over > 0):
                with sp.Fori(1, PASSES) as c:
                    with sp.Fori(0, BODIES) as n:
                        for i in range(2):
                            load_pair(c * BODIES + n, i, n * 2 + i)
            for t in range(T):
                for nh in range(NH):
                    r = slice(nh * HALF, (nh + 1) * HALF)
                    sp.wait_ge(sem("out_ready"), T * t + nh + 1)
                    sp.dma_start(out_dram[:, t, r], x[:, t, r]).then_inc(sem("out_sent"), 16)
            sp.wait_ge(sem("out_sent"), 16 * T * NH)

        @block.gpsimd
        def _(pool):
            pool.memset(expo[:], -0.5).then_inc(sem("expo_set"), 1)
            pool.memset(scT, 0.0).then_inc(sem("scT_zero"), 1)
            pool.memset(lv[3], 1.0).then_inc(sem("resets"), 1)
            pool.wait_ge(sem("resets"), 1)
            pool.memset(lv[3].rearrange("p (n c) -> p n c", c=CHUNK)[:, :, 0:1], 0.0).then_inc(sem("resets"), 1)
            pool.memset(table[:], -1.0).then_inc(sem("table_set"), 1)
            pool.wait_ge(sem("expo_set"), 1)

            def rsqrt(o, i, n, name):
                for t in range(T):
                    pool.wait_ge(sem(f"{name}_mean"), t + 1)
                    pool.tensor_tensor(o[:, n * t:n * (t + 1)], i[:, n * t:n * (t + 1)], expo[:, 0:n],
                                       ALU.pow).then_inc(sem(f"{name}_rstd"), 1)

            rsqrt(rstd, ms, 1, "norm1")
            rsqrt(rstd, ms, HEADS, "head")
            rsqrt(rstdb, msb, 1, "norm2")
            for k in range(1, len(aside)):
                from_aside(pool, k)
            rsqrt(rstdc, msc, 1, "normf")

        @block.scalar
        def _(act):
            def dma(dst, src, name):
                act.dma_start(dst, src, allow_slow_non_contiguous=True).then_inc(sem(name), 16)

            act.wait_ge(sem("expo_set"), 1)
            act.activation(expo2[:], expo[:], ACT.Square).then_inc(sem("squared"), 1)
            dma(consts[:, 0:P], A["consts"][:, 0:P], "ident_in")
            dma(g1[:], A["norm1_g"][0].rearrange("(c p) -> p c", p=P), "g1_in")
            for r in range(2):
                dma(lbr[:, r, :], A["hgrn_lb"][r].rearrange("(c p) -> p c", p=P), "lb_in")
            for t in range(T):
                act.wait_ge(sem(f"x_in{t}"), 16)
                act.activation(lv[t], x[:, t, :], ACT.Square, accum_out=ss[:, t:t + 1]).then_inc(sem("norm1_sum"), 1)
            act.wait_ge(sem("lb_diff"), 1)
            act.activation(lb[:], two[:], ACT.Sigmoid).then_inc(sem("lb_ready"), 1)
            dma(consts[:, P:], A["consts"][:, P:], "consts_in")
            dma(pool_w[:], A["pool_w"][0].rearrange("g c d -> c g d"), "rest_in")
            dma(pool_s[:], A["pool_scale"][0].rearrange("(c p) -> p c", p=P), "rest_in")
            dma(hnorm[:], A["hgrn_norm_g"].rearrange("o p -> p o"), "rest_in")
            dma(g2[:], A["norm2_g"][0].rearrange("(c p) -> p c", p=P), "rest_in")
            dma(router[:], A["router_w"][0].rearrange("(c p) e -> p c e", p=P), "rest_in")
            dma(rbias[:], A["router_b"].to_broadcast([P, E]), "rest_in")
            for b in range(2):
                product_done(act, "f_done", b, 0)
                act.activation(fs[:, b * HALF:(b + 1) * HALF], bank[4 + b][:], ACT.Sigmoid).then_inc(sem("f_sig"), 1)
            act.wait_ge(sem("k_ready"), 1)
            act.activation(fs, fs, ACT.Ln).then_inc(sem("logf_ready"), 1)
            for b in range(2):
                product_done(act, "q_done", b, 1)
                act.activation(lv[0][:, b * HALF:(b + 1) * HALF], bank[6 + b][:], ACT.Sigmoid).then_inc(sem("q_sig"), 1)

            def level_exp(n):
                act.wait_ge(sem("diff_ready"), n + 1)
                act.activation(lv[n % 4], lv[n % 4], ACT.Exp).then_inc(sem("decay_ready"), 1)

            for n in range(4):
                level_exp(n)
            for t in range(T):
                product_done(act, "v_done", t, 2)
                act.copy(vv[:, t, :], bank[t][:]).then_inc(sem("v_ready"), 1)
            for n in range(4, 6):
                level_exp(n)
            act.wait_ge(sem("scored"), 3)
            act.copy(scX.rearrange("p h t -> p (h t)"), bank[4][:]).then_inc(sem("coarse_ready"), 1)
            act.wait_ge(sem("scT_zero"), 1)
            act.copy(scT[0:64, :, 64:128], bank[5][0:64, :].rearrange("p (a t) -> p a t", a=8)).then_inc(sem("coarse_ready"), 1)
            for a in range(2):
                act.copy(scT[64 * a:64 * a + 32, :, 64 * a + 32:64 * a + 64],
                         bank[6][64 * a:64 * a + 32, 0:256].rearrange("p (a t) -> p a t", a=8)).then_inc(sem("coarse_ready"), 1)
            for n in range(6, 8):
                level_exp(n)
            for b in range(2):
                product_done(act, "u_done", b, 3)
                act.copy(uu[:, 2 * b:2 * b + 2, :], bank[2 + b][:].rearrange("p (g t) -> p g t", g=2)).then_inc(sem("u_ready"), 1)
            for t in range(T):
                product_done(act, "g_done", t, 4)
                act.activation(sigg[:, t, :], bank[t][:], ACT.Sigmoid).then_inc(sem("g_sig"), 1)
            act.wait_ge(sem("rest_in"), 96)
            for g in range(HEADS):
                act.wait_ge(sem("pool_done"), g // 2 + 1)
                act.activation(ocT[:, HEADS + g, :], bank[2 + g // 2][:, g % 2 * SEQ:(g % 2 + 1) * SEQ], ACT.Copy,
                               scale=pool_s[:, g:g + 1]).then_inc(sem("pooled_ready"), 1)
            for t in range(T):
                act.wait_ge(sem("o_done"), t + 1)
                act.activation(osq[:, t, :], bank[6 + t][:], ACT.Square).then_inc(sem("o_squares"), 1)
            for h in range(HEADS):
                act.wait_ge(sem("oT_done"), h // 2 + 1)
                act.activation(ocT[:, h, :], bank[4 + h // 2][:, h % 2 * SEQ:(h % 2 + 1) * SEQ], ACT.Copy,
                               scale=hnorm[:, 0:1]).then_inc(sem("heads_ready"), 1)

            for m, name in enumerate(("b_gate", "b_up", "b_down")):
                dma(bias[m * E:(m + 1) * E, :], A[name][0], "bias_in")
            dma(bias[3 * E:3 * E + 1, :], A["norm_f_g"].rearrange("(o d) -> o d", o=1), "normf_in")
            for k in (0, 1, 3):
                load_aside(act, k)
            for q in range(T * NH):
                act.wait_ge(sem("mixed"), q + 1)
                r = slice(q % NH * HALF, (q % NH + 1) * HALF)
                act.activation(hn[:, q // NH, r], x[:, q // NH, r], ACT.Square,
                               accum_out=ssb[:, q:q + 1]).then_inc(sem("norm2_sum"), 1)
                if q % NH:
                    t = q // NH
                    act.wait_ge(sem("norm2_rstd"), t + 1)
                    act.activation(hn[:, t, :], x[:, t, :], ACT.Copy, scale=rstdb[:, t:t + 1]).then_inc(sem("rows_ready"), 1)
            for t in range(T):
                act.wait_ge(sem("top_ready"), t + 1)
                act.activation(prob[:, t, :], top[:, t, 0:TOPK], ACT.Exp, bias=ntop[:, t:t + 1],
                               accum_out=psum_[:, t:t + 1]).then_inc(sem("prob_ready"), 1)
            load_aside(act, 2)
            load_aside(act, 4)
            act.wait_ge(sem("gate_ready"), 1)
            for c in range(1, PASSES):
                act.copy(table[:, T:2 * T, c * E:(c + 1) * E], table[:, T:2 * T, 0:E]).then_inc(sem("gates_ready"), 1)

            def pair_steps(n, i, pair):
                p = n * 2 + i
                act.wait_ge(sem("gt_ready"), p * 2 + 2)
                act.wait_ge(sem("gated"), AHEAD + p)
                act.activation(sg, gt, ACT.Sigmoid, scale=ALPHA).then_inc(sem("sg_ready"), 1)
                aside_used(act, 2)
                act.wait_ge(sem("combined"), AHEAD + p * 4)
                act.wait_ge(sem("gtT_done"), p + 1)
                act.copy(gtT, bank[0][:, 0:T * P]).then_inc(sem("gtT_ready"), 1)
                for h in range(2):
                    act.wait_ge(sem("actT_done"), p * 2 + h + 1)
                    act.copy(actT[:, 4 * h:4 * h + 4, :], bank[h][:].rearrange("p (c s) -> p c s", c=4)).then_inc(sem("actT_ready"), 1)
                act.wait_ge(sem("half_done"), p * 3 + 3)
                act.copy(yy[:, 0:HALF], bank[4][:]).then_inc(sem("y0_ready"), 1)

            over = overflowed(act)
            with act.Fori(0, BODIES) as n:
                for i in range(2):
                    pair_steps(n, i, n * 2 + i)
            with act.If(over > 0):
                with act.Fori(1, PASSES) as c:
                    with act.Fori(0, BODIES) as n:
                        for i in range(2):
                            pair_steps(c * BODIES + n, i, n * 2 + i)
                act.wait_ge(sem("added"), AHEAD + PASSES * PAIRS * 4)
            for q in range(T * NH):
                act.wait_ge(sem("added"), AHEAD + PAIRS * 4 - T * NH + q + 1)
                t, r = q % T, slice(q // T * HALF, (q // T + 1) * HALF)
                act.activation((gt, sg)[t][:, r], x[:, t, r], ACT.Square,
                               accum_out=ssc[:, NH * t + q // T:NH * t + q // T + 1]).then_inc(sem("normf_sum"), 1)

        @block.tensor
        def _(pe):
            def mm(o, l, r, first, last):
                return pe.matmul(o, l, r, start=first, stop=last)

            def turn(rows, t, h, b0, name):
                for c in range(4):
                    ins = pe.transpose(bank[b0 + 2 * t + h][:, c * P:(c + 1) * P],
                                       rows[:, t, (4 * h + c) * P:(4 * h + c + 1) * P], ident)
                    if c == 2 and b0 == 0 and t == 0 and h == 0:
                        ins.then_inc(ring_read, AHEAD)
                ins.then_inc(sem(name), 1)

            def keep_clock(n, b, operand):
                for _ in range(n):
                    mm(bank[b][:, 0:P], operand, operand, True, True)

            pe.wait_ge(sem("scT_zero"), 1)
            keep_clock(12, 7, scT[:, 0, :])
            pe.wait_ge(sem("ident_in"), 16)
            for h in range(2):
                for t in range(T):
                    pe.wait_ge(sem("hn_ready"), t + 1)
                    turn(hn, t, h, 0, "hT_done")

            def columns_first(s, b0, name, between=None):
                w = front_block(s)
                if s:
                    pe.wait_ge(sem(f"front_in{s}"), 16)
                for m in range(HEADS):
                    if s == 0 and m % 2 == 0:
                        pe.wait_ge(sem(f"front_in0_{m // 2}"), 16)
                    if m == 2 and between:
                        between()
                    for c in range(KC):
                        if s == 0 and m == 0 and c % 4 == 0:
                            pe.wait_ge(sem("hT_ready"), 2 + 2 * (c // 4))
                        if c == KC - 1 and m == HEADS - 1:
                            ins.then_inc(ring_read, 1)
                        ins = mm(bank[b0 + m // 2][:, m % 2 * SEQ:(m % 2 + 1) * SEQ], w[:, c, m * P:(m + 1) * P],
                                 hT[:, c, :], c == 0, c == KC - 1)
                    if m % 2:
                        ins.then_inc(ring_read if m == HEADS - 1 else sem(name), 1)

            def tokens_first(s, name):
                w = front_block(s)
                pe.wait_ge(sem(f"front_in{s}"), 16)
                for t in range(T):
                    for c in range(KC):
                        if c == KC - 1 and t == T - 1:
                            ins.then_inc(ring_read, 1)
                        ins = mm(bank[t][:], hT[:, c, t * P:(t + 1) * P], w[:, c, :], c == 0, c == KC - 1)
                    ins.then_inc(ring_read if t == T - 1 else sem(name), 1)

            def score(n):
                half = LEVELS[n] if n < len(LEVELS) else 0
                if half:
                    pe.wait_ge(sem("level_ready"), n + 1)
                    m = lv[n % 4].rearrange("p (h t) -> p h t", h=HEADS)
                    keys, queries = m, m
                else:
                    keys, queries = (b.rearrange("p (h t) -> p h t", h=HEADS) for b in (ks, qs))
                for h in range(HEADS):
                    if half == 128:
                        ins = mm(bank[4][:, h * P:(h + 1) * P], keys[:, h, 0:P], queries[:, h, P:2 * P], True, True)
                        continue
                    for t in range(T):
                        a = h * T + t
                        if half == 64:
                            ins = mm(bank[5][0:64, a * 64:(a + 1) * 64], keys[:, h, t * P:t * P + 64],
                                     queries[:, h, t * P + 64:t * P + 128], True, True)
                        elif half == 32:
                            for b in range(2):
                                o = t * P + 64 * b
                                ins = mm(bank[6][64 * b:64 * b + 32, a * 32:(a + 1) * 32], keys[:, h, o:o + 32],
                                         queries[:, h, o + 32:o + 64], True, True)
                        else:
                            bk, c0 = {3: (7, 0), 4: (7, 256), 5: (4, 0), 6: (4, 256), 7: (5, 0), 8: (5, 256)}[n]
                            for b in range(4):
                                o = t * P + 32 * b
                                ins = mm(bank[bk][32 * b:32 * b + 32, c0 + a * 32:c0 + (a + 1) * 32],
                                         keys[:, h, o:o + 32], queries[:, h, o:o + 32], True, True)
                ins.then_inc(sem("scored"), 1)

            columns_first(0, 4, "f_done")
            columns_first(1, 6, "q_done")
            tokens_first(2, "v_done")
            for n in range(3):
                score(n)
            columns_first(3, 2, "u_done", lambda: score(3))
            score(4)
            pe.wait_ge(sem("coarse_ready"), 4)
            for n in range(5, 9):
                score(n)
            pe.wait_ge(sem("v_ready"), 2)
            tokens_first(4, "g_done")
            pe.wait_ge(sem("rest_in"), 96)
            pe.wait_ge(sem("consts_in"), 16)
            for g in range(HEADS):
                pe.wait_ge(sem("pool_in"), g + 1)
                pe.wait_ge(sem("u_ready"), 2)
                ins = mm(bank[2 + g // 2][:, g % 2 * SEQ:(g % 2 + 1) * SEQ], pool_w[:, g, :], uu[:, g, :], True, True)
                if g % 2:
                    ins.then_inc(sem("pool_done"), 1)
            pe.wait_ge(sem("diag_ready"), 4)
            for t in range(T):
                for h in range(HEADS):
                    o = bank[6 + t][:, h * P:(h + 1) * P]
                    v_h = [vv[:, u, h * P:(h + 1) * P] for u in range(T)]
                    ins = mm(o, scT[:, h * T + t, :], v_h[t], True, t == 0)
                    if t:
                        ins = mm(o, scX[:, h, :], v_h[0], False, True)
                ins.then_inc(sem("o_done"), 1)
            def w_out_rows(t, nh, s, between=None):
                rows, c0 = w_out_half(s), 4 if s == 5 else 0
                for c in range(4):
                    if t == T - 1 and nh == NH - 1 and c == 3:
                        ins.then_inc(ring_read, 1)
                    if c == 1 and between:
                        between()
                    ins = mm(bank[2 * t + nh][:], ocT[:, c0 + c, t * P:(t + 1) * P],
                             rows[:, c, nh * HALF:(nh + 1) * HALF], s == 5 and c == 0, s == 6 and c == 3)
                return ins

            pe.wait_ge(sem("front_in5"), 16)
            pe.wait_ge(sem("gg_ready"), 2)
            for nh in range(NH):
                pe.wait_ge(sem("pooled_ready"), 4)
                w_out_rows(0, nh, 5)
            for t in range(T):
                pe.wait_ge(sem("o_ready"), t + 1)
                for h in range(HEADS):
                    ins = pe.transpose(bank[4 + h // 2][:, h % 2 * SEQ + t * P:h % 2 * SEQ + (t + 1) * P],
                                       ob[:, t, h * P:(h + 1) * P], ident)
                    if t and h % 2:
                        ins.then_inc(sem("oT_done"), 1)
            for nh in range(NH):
                ins = w_out_rows(1, nh, 5)
            ins.then_inc(ring_read, 1)
            pe.wait_ge(sem("front_in6"), 16)
            pe.wait_ge(sem("heads_ready"), HEADS)
            for nh in range(NH):
                w_out_rows(0, nh, 6).then_inc(sem("proj_done"), 1)
            w_out_rows(1, 0, 6).then_inc(sem("proj_done"), 1)

            def bias_rows(i, m, b0, halves=range(NH)):
                for nh in halves:
                    mm(bank[b0 + nh][:], which[m * E:(m + 1) * E, i, :],
                       bias[m * E:(m + 1) * E, nh * HALF:(nh + 1) * HALF], True, False)

            def route(t):
                for c in range(KC):
                    if c % 4 == 0:
                        pe.wait_ge(sem("hT2_ready"), 2 * t + c // 4 + 1)
                    g = c % 4
                    ins = mm(bank[2 + t][g * E:(g + 1) * E, 0:P], router[:, c, :], hT[:, c, t * P:(t + 1) * P],
                             c < 4, c >= 4)
                ins.then_inc(sem("parts_done"), 1)

            def turn_logits(t):
                pe.wait_ge(sem("parts_ready"), t + 1)
                mm(bank[2 + t][:, P:P + E], parts[:, t, :], thrice, True, True).then_inc(sem("logits_done"), 1)

            def bias_rows(i, m, b0, halves=range(NH)):
                for nh in halves:
                    mm(bank[b0 + nh][:], which[m * E:(m + 1) * E, i, :],
                       bias[m * E:(m + 1) * E, nh * HALF:(nh + 1) * HALF], True, False)

            for q in range(3):
                pe.wait_ge(sem("mixed"), q + 1)
                turn(x, q // 2, q % 2, 4, "hT2_done")
            route(0)
            w_out_rows(1, 1, 6, lambda: turn_logits(0)).then_inc(ring_read, 1)
            pe.wait_ge(sem("which_ready"), 1)
            pe.wait_ge(sem("bias_in"), 48)
            bias_rows(0, 0, 0, (0,))
            pe.wait_ge(sem("mixed"), 4)
            turn(x, 1, 1, 4, "hT2_done")
            bias_rows(0, 0, 0, (1,))
            route(1)
            keep_clock(1, 6, ones)
            turn_logits(1)
            pe.wait_ge(sem("chosen_ready"), 1)
            mm(bank[4][:, 0:E], before, chosen[:, 0, :], True, True)
            mm(bank[4][:, E:2 * E], ones, chosen[:, 0, :], True, False)
            keep_clock(6, 6, ones)
            pe.wait_ge(sem("chosen_ready"), 2)
            mm(bank[4][:, E:2 * E], before, chosen[:, 1, :], False, True).then_inc(sem("pos_done"), 1)
            mm(bank[5][:, 0:E], ones, chosen[:, 0, :], True, False)
            mm(bank[5][:, 0:E], ones, chosen[:, 1, :], False, True).then_inc(sem("count_done"), 1)
            keep_clock(2, 6, ones)

            def gather():
                for c in range(KC):
                    for t in range(T):
                        ins = mm(bank[6 + c // 4][:, c % 4 * P:(c % 4 + 1) * P], hn[:, t, c * P:(c + 1) * P],
                                 pick[:, t, :], t == 0, t == T - 1)
                    if c % 4 == 3:
                        ins.then_inc(sem("gathered"), 1)

            pe.wait_ge(sem("pick_ready"), 1)
            pe.wait_ge(sem("rows_ready"), 2)
            gather()

            def product(n, i, m, b0, lhs, operand, between={}):
                for k in range(QUARTERS):
                    j = 2 * QUARTERS * m + 2 * k
                    if k in between:
                        between[k]()
                    for e in range(2):
                        pe.wait_ge(landed[slot_of(i, j + e)], landed_at(n, i, j + e))
                    if k % 2 == 0:
                        operand(k // 2)
                    rows = range(ROWS * k, ROWS * (k + 1))
                    order = [(nh, c) for nh in range(NH) for c in rows]
                    if row_by_row(CPP * i + j):
                        order = [(nh, c) for c in rows for nh in range(NH)]
                    for nh, c in order:
                        if c % ROWS and nh == 0 and row_by_row(CPP * i + j):
                            for e in range(2):
                                pe.wait_ge(sem(f"last_row{e}"), n * 16 + 16)
                        for e in range(2):
                            r = slice(e * SLOTS, (e + 1) * SLOTS)
                            ins = mm(bank[b0 + nh][r, :], lhs[:, c, r],
                                     ring[:, slot_of(i, j + e), c % ROWS, nh * HALF:(nh + 1) * HALF],
                                     False, c == KC - 1)
                            if c % ROWS == ROWS - 1 and nh == NH - 1:
                                ins.then_inc(ring_read, 1)
                        if c == KC - 1 and nh == 0:
                            ins.then_inc(sem("half_done"), 1)

            def pair_steps(n, i, pair):
                p = n * 2 + i
                product(n, i, 0, 0, xsT[i], lambda h: pe.wait_ge(sem("xs_ready"), p * 2 + h + 1))

                def gates_turned():
                    pe.wait_ge(sem("gt_ready"), p * 2 + 2)
                    pe.wait_ge(sem("pickg_ready"), p + 1)
                    for t in range(T):
                        ins = pe.transpose(bank[0][:, t * P:(t + 1) * P], pickg[:, t, :], ident)
                    ins.then_inc(sem("gtT_done"), 1)

                def next_rows():
                    pe.wait_ge(sem("pick_ready"), p + 2)
                    pe.wait_ge(sem("added"), AHEAD + p * 4)
                    gather()

                pe.wait_ge(sem("up_read"), AHEAD + p * 2)
                bias_rows(i, 1, 2)
                product(n, i, 1, 2, xsT[i], lambda h: None, {2: gates_turned, 3: next_rows})
                bias_rows(i, 2, 4)
                pe.wait_ge(sem("gtT_ready"), p + 1)
                for h in range(2):
                    pe.wait_ge(sem("act_ready"), p * 2 + h + 1)
                    for c in range(4):
                        ins = pe.transpose(bank[h][:, c * P:(c + 1) * P],
                                           up[:, (4 * h + c) * P:(4 * h + c + 1) * P], ident)
                    ins.then_inc(sem("actT_done"), 1)

                def next_gate_bias():
                    pe.wait_ge(sem("actT_ready"), p * 2 + 2)
                    bias_rows(1 - i, 0, 0)

                product(n, i, 2, 4, actT, lambda h: pe.wait_ge(sem("actT_ready"), p * 2 + h + 1), {2: next_gate_bias})
                pe.wait_ge(sem("xs_ready"), p * 2 + 4)
                for nh in range(NH):
                    pe.wait_ge(sem(f"y{nh}_ready"), p + 1)
                    for t in range(T):
                        mm(bank[6 - 2 * nh + t][:], gtT[:, t * P:(t + 1) * P], yy[:, nh * HALF:(nh + 1) * HALF],
                           True, True).then_inc(sem("combined"), 1)

            with pe.Fori(0, BODIES) as n:
                for i in range(2):
                    pair_steps(n, i, n * 2 + i)
            over = overflowed(pe)
            with pe.If(over > 0):
                with pe.Fori(1, PASSES) as c:
                    with pe.Fori(0, BODIES) as n:
                        for i in range(2):
                            pair_steps(c * BODIES + n, i, n * 2 + i)
            pe.wait_ge(sem("normf_in"), 16)
            for nh in range(NH):
                mm(bank[2 + nh][:], ones[3 * E:3 * E + 1, :], bias[3 * E:3 * E + 1, nh * HALF:(nh + 1) * HALF],
                   True, True).then_inc(sem("normf_wide"), 1)

        @block.vector
        def _(dve):
            steps = [0]

            def seq(ins):
                steps[0] += 1
                ins.then_inc(sem("dve_step"), 1)
                dve.wait_ge(sem("dve_step"), steps[0])

            def ahead(ins, name):
                ins.then_inc(sem(name), AHEAD)
                dve.wait_ge(sem(name), AHEAD)

            def mean(o, i, scale, name):
                dve.tensor_scalar(o, i, scale, EPS, ALU.mult, ALU.add).then_inc(sem(name), 1)

            for t in range(T):
                dve.wait_ge(sem("norm1_sum"), t + 1)
                mean(ms[:, t:t + 1], ss[:, t:t + 1], 1.0 / D, "norm1_mean")
            for t in range(T):
                dve.wait_ge(sem("norm1_rstd"), t + 1)
                dve.tensor_scalar(hn[:, t, :], x[:, t, :], rstd[:, t:t + 1], None, ALU.mult).then_inc(sem("hn_ready"), 1)

            def from_turned(t, h, b0, g, done, count, name):
                dve.wait_ge(sem(done), count)
                dve.tensor_tensor(hT[:, 4 * h:4 * h + 4, t * P:(t + 1) * P],
                                  bank[b0 + 2 * t + h][:].rearrange("p (c t) -> p c t", c=4),
                                  g[:, 4 * h:4 * h + 4].unsqueeze(2).broadcast_to([P, 4, P]),
                                  ALU.mult).then_inc(sem(name), 1)

            dve.wait_ge(sem("g1_in"), 16)
            for h in range(2):
                for t in range(T):
                    from_turned(t, h, 0, g1, "hT_done", T * h + t + 1, "hT_ready")
            dve.wait_ge(sem("lb_in"), 32)
            dve.tensor_tensor(two[:], lbr[:, 0, :], lbr[:, 1, :], ALU.subtract).then_inc(sem("lb_diff"), 1)
            dve.wait_ge(sem("lb_ready"), 1)
            seq(dve.tensor_scalar(oml[:], lb[:], -1.0, 1.0, ALU.mult, ALU.add))
            for h in range(HEADS):
                dve.wait_ge(sem("f_sig"), h // 2 + 1)
                ins = dve.tensor_scalar(fs[:, h * SEQ:(h + 1) * SEQ], fs[:, h * SEQ:(h + 1) * SEQ], oml[:, h:h + 1],
                                        lb[:, h:h + 1], ALU.mult, ALU.add)
                seq(ins)
            dve.tensor_scalar(ks, fs, -1.0, 1.0, ALU.mult, ALU.add).then_inc(sem("k_ready"), 1)
            dve.wait_ge(sem("resets"), 2)
            dve.wait_ge(sem("logf_ready"), 1)
            seq(dve.tensor_tensor_scan(bs, lv[3], fs, 0.0, ALU.mult, ALU.add))
            for b in range(2):
                dve.wait_ge(sem("q_sig"), b + 1)
                r = slice(b * HALF, (b + 1) * HALF)
                seq(dve.tensor_tensor(qs[:, r], bank[6 + b][:], lv[0][:, r], ALU.mult))

            kv, qv = ks, qs
            b4 = bs.rearrange("p (h c t) -> p h c t", h=HEADS, c=4)
            k4 = ks.rearrange("p (h c t) -> p h c t", h=HEADS, c=4)
            seq(dve.tensor_tensor(two[:], b4[:, :, 0, CHUNK - 1], b4[:, :, 1, CHUNK - 1], ALU.add))

            def wide(a):
                return a.broadcast_to([P, HEADS, CHUNK])

            for n, half in enumerate(LEVELS):
                m = lv[n % 4]
                m4 = m.rearrange("p (h c t) -> p h c t", h=HEADS, c=4)
                if n >= 4:
                    dve.wait_ge(sem("scored"), n - 3)
                if half == 128:
                    dve.tensor_tensor(m4[:, :, 0, :], wide(two[:].unsqueeze(2)), b4[:, :, 0, :], ALU.subtract)
                    dve.tensor_tensor(m4[:, :, 1, :], wide(b4[:, :, 1, CHUNK - 1:]), b4[:, :, 1, :], ALU.subtract)
                    dve.tensor_copy(m4[:, :, 2, :], b4[:, :, 2, :])
                    last = dve.tensor_tensor(m4[:, :, 3, :], b4[:, :, 3, :], wide(b4[:, :, 2, CHUNK - 1:]), ALU.add)
                elif half == 64:
                    for c in (0, 2):
                        dve.tensor_tensor(m4[:, :, c, :], wide(b4[:, :, c, CHUNK - 1:]), b4[:, :, c, :], ALU.subtract)
                        last = dve.tensor_copy(m4[:, :, c + 1, :], b4[:, :, c + 1, :])
                else:
                    bl, ml = lvl(bs, half), lvl(m, half)
                    blocks = HEADS * SEQ // (2 * half)
                    ref = bl[:, :, 0, half - 1:].broadcast_to([P, blocks, half])
                    dve.tensor_tensor(ml[:, :, 0, :], ref, bl[:, :, 0, :], ALU.subtract)
                    last = dve.tensor_tensor(ml[:, :, 1, :], bl[:, :, 1, :], ref, ALU.subtract)
                last.then_inc(sem("diff_ready"), 1)

                def finish(n):
                    half = LEVELS[n]
                    dve.wait_ge(sem("decay_ready"), n + 1)
                    ml, kl, ql = lvl(lv[n % 4], half), lvl(ks, half), lvl(qs, half)
                    dve.tensor_tensor(ml[:, :, 0, :], ml[:, :, 0, :], kl[:, :, 0, :], ALU.mult)
                    dve.tensor_tensor(ml[:, :, 1, :], ml[:, :, 1, :], ql[:, :, 1, :], ALU.mult).then_inc(sem("level_ready"), 1)

                if n:
                    finish(n - 1)
            finish(len(LEVELS) - 1)

            dve.wait_ge(sem("consts_in"), 16)
            seq(dve.memset(fs[:, 0:SEQ], 1.0))
            for g in range(HEADS):
                dve.wait_ge(sem("u_ready"), g // 2 + 1)
                ins = dve.tensor_tensor_scan(cs[:, g, :], fs[:, 0:SEQ], uu[:, g, :], 0.0, ALU.mult, ALU.add)
            seq(ins)
            for g, w in enumerate(WINDOWS):
                ins = dve.scalar_tensor_tensor(uu[:, g, w:], cs[:, g, 0:SEQ - w], 1.0 / w, uu[:, g, w:], ALU.mult, ALU.add)
            seq(ins)
            seq(dve.tensor_tensor(cs[:, :, 0:short.shape[2]], cs[:, :, 0:short.shape[2]], short, ALU.mult))
            for g, w in enumerate(WINDOWS):
                dve.scalar_tensor_tensor(uu[:, g, :], cs[:, g, :], 1.0 / w, uu[:, g, :], ALU.mult,
                                         ALU.subtract).then_inc(sem("pool_in"), 1)
            dve.wait_ge(sem("scored"), 9)
            for l, (bk, c0) in enumerate(((7, 0), (7, 256), (4, 0), (4, 256), (5, 0), (5, 256))):
                ins = dve.tensor_tensor(picked[:, l, :].rearrange("p (a t) -> p a t", a=8),
                                        bank[bk][:, c0:c0 + 256].rearrange("p (a t) -> p a t", a=8),
                                        masks[:, l, :].unsqueeze(1).broadcast_to([P, 8, SMALL]), ALU.mult)
            seq(ins)
            fine = lv[0][:, 0:256]
            seq(dve.tensor_reduce(fine, picked.rearrange("p l x -> p x l"), AX.X, ALU.add))
            for b in range(4):
                r = slice(32 * b, 32 * b + 32)
                dve.tensor_copy(scT[r, :, r], fine[r, :].rearrange("p (a t) -> p a t", a=8)).then_inc(sem("diag_ready"), 1)
            for t in range(T):
                dve.wait_ge(sem("g_sig"), t + 1)
                dve.tensor_tensor(gg[:, t, :], bank[t][:], sigg[:, t, :], ALU.mult).then_inc(sem("gg_ready"), 1)
            for t in range(T):
                dve.wait_ge(sem("o_squares"), t + 1)
                seq(dve.tensor_reduce(ss[:, 4 * t:4 * t + 4], osq[:, t, :].rearrange("p (h v) -> p h v", h=HEADS), AX.X, ALU.add))
                mean(ms[:, 4 * t:4 * t + 4], ss[:, 4 * t:4 * t + 4], 1.0 / P, "head_mean")
            dve.wait_ge(sem("gg_ready"), 2)
            for t in range(T):
                dve.wait_ge(sem("head_rstd"), t + 1)
                o3 = ob[:, t, :].rearrange("p (h v) -> p h v", h=HEADS)
                seq(dve.tensor_tensor(o3, bank[6 + t][:].rearrange("p (h v) -> p h v", h=HEADS),
                                      rstd[:, 4 * t:4 * t + 4].unsqueeze(2).broadcast_to([P, HEADS, P]), ALU.mult))
                dve.tensor_tensor(ob[:, t, :], ob[:, t, :], gg[:, t, :], ALU.mult).then_inc(sem("o_ready"), 1)
            def add_mixed(t, nh):
                r = slice(nh * HALF, (nh + 1) * HALF)
                if t and nh:
                    dve.wait_ge(ring_read, AHEAD + FRONT)
                else:
                    dve.wait_ge(sem("proj_done"), 2 * t + nh + 1)
                dve.tensor_tensor(x[:, t, r], bank[2 * t + nh][:], x[:, t, r], ALU.add).then_inc(sem("mixed"), 1)

            def mean_of_halves(o, i, t, name, sums):
                dve.wait_ge(sem(f"{name}_sum"), sums)
                seq(dve.tensor_tensor(i[:, 2 * t:2 * t + 1], i[:, 2 * t:2 * t + 1], i[:, 2 * t + 1:2 * t + 2], ALU.add))
                mean(o[:, t:t + 1], i[:, 2 * t:2 * t + 1], 1.0 / D, f"{name}_mean")

            def logit_parts(t):
                dve.wait_ge(sem("parts_done"), t + 1)
                dve.tensor_copy(parts[:, t, :], bank[2 + t][:, 0:P]).then_inc(sem("parts_ready"), 1)

            def choose_experts(t):
                dve.wait_ge(sem("logits_done"), t + 1)
                dve.wait_ge(sem("norm2_rstd"), t + 1)
                seq(dve.scalar_tensor_tensor(logits[:, t, :], bank[2 + t][:, P:P + E], rstdb[:, t:t + 1], rbias[:],
                                             ALU.mult, ALU.add))
                seq(dve.max(top[:, t, :], logits[:, t, :]))
                seq(dve.max_index(topi[:, t, :], top[:, t, :], logits[:, t, :]))
                h = hit[:, t * TOPK:(t + 1) * TOPK, :]
                seq(dve.tensor_tensor(h, expert_no.unsqueeze(1).broadcast_to([P, TOPK, E]),
                                      topi[:, t, 0:TOPK].unsqueeze(2).broadcast_to([P, TOPK, E]),
                                      ALU.is_equal))
                dve.tensor_reduce(chosen[:, t, :], h.rearrange("p k e -> p e k"), AX.X, ALU.add).then_inc(sem("chosen_ready"), 1)
                dve.tensor_scalar(ntop[:, t:t + 1], top[:, t, 0:1], -1.0, None, ALU.mult).then_inc(sem("top_ready"), 1)

            def place_tokens():
                dve.wait_ge(sem("pos_done"), 1)
                dve.wait_ge(sem("chosen_ready"), 2)
                seq(dve.scalar_tensor_tensor(posn[:], bank[4][:, 0:2 * E].rearrange("p (t e) -> p t e", t=T), 1.0,
                                             chosen[:], ALU.add, ALU.mult))
                seq(dve.tensor_scalar(table[:, 0:T, 0:E], posn[:], -1.0, None, ALU.add))
                pick_slots(0, table[:, 0, 0:2])
                pick_slots(1, table[:, 1, 0:2]).then_inc(sem("pick_ready"), 1)

            def pick_slots(t, pos):
                return dve.tensor_tensor(pick[:, t, :].rearrange("p (e s) -> p e s", e=2),
                                         slot_no.unsqueeze(1).broadcast_to([P, 2, SLOTS]),
                                         pos.unsqueeze(2).broadcast_to([P, 2, SLOTS]), ALU.is_equal)

            def pick_rows(i, first):
                return dve.tensor_copy(which[:, i, :].rearrange("q (e s) -> q e s", e=2),
                                       thrice[0:3 * E, bass.ds(first, 2)].unsqueeze(2).broadcast_to([3 * E, 2, SLOTS]))

            def pick_gates(pos, gates):
                for t in range(T):
                    for e in range(2):
                        b = dve.tensor_scalar(pickg[:, t, e * SLOTS:(e + 1) * SLOTS], slot_no, pos[:, t, e:e + 1],
                                              gates[:, t, e:e + 1], ALU.is_equal, ALU.mult)
                b.then_inc(sem("pickg_ready"), 1)

            dve.wait_ge(sem("rest_in"), 96)
            dve.wait_ge(sem("table_set"), 1)
            dve.wait_ge(sem("consts_in"), 16)
            pick_rows(0, 0).then_inc(sem("which_ready"), 1)
            for nh in range(NH):
                add_mixed(0, nh)
            mean_of_halves(msb, ssb, 0, "norm2", NH)
            add_mixed(1, 0)
            for h in range(2):
                from_turned(0, h, 4, g2, "hT2_done", h + 1, "hT2_ready")
            from_turned(1, 0, 4, g2, "hT2_done", 3, "hT2_ready")
            logit_parts(0)
            choose_experts(0)
            add_mixed(1, 1)
            from_turned(1, 1, 4, g2, "hT2_done", 4, "hT2_ready")
            mean_of_halves(msb, ssb, 1, "norm2", 2 * NH)
            logit_parts(1)
            choose_experts(1)
            place_tokens()
            dve.wait_ge(sem("prob_ready"), 2)
            seq(dve.reciprocal(rps[:], psum_[:]))
            ahead(dve.tensor_tensor(prob[:], prob[:], rps[:].unsqueeze(2).broadcast_to([P, T, TOPK]), ALU.mult), "gated")
            ahead(dve.tensor_tensor(hitg[:], hit[:],
                                    prob[:].rearrange("p t k -> p (t k)").unsqueeze(2).broadcast_to([P, T * TOPK, E]),
                                    ALU.mult), "combined")
            dve.tensor_reduce(table[:, T:2 * T, 0:E], hitg[:].rearrange("p (t k) e -> p t e k", t=T), AX.X,
                              ALU.add).then_inc(sem("gate_ready"), 1)

            def choose(p, i, pair):
                dve.tensor_copy(cur[:], table[:, :, bass.ds(p * 2 + 2, 2)]).then_inc(sem("cur_ready"), 1)
                dve.wait_ge(sem("cur_ready"), p + 1)
                pick_rows(1 - i, dve.snap((pair + 1) % PAIRS * 2))
                for t in range(T):
                    a = pick_slots(t, cur[:, t, :])
                a.then_inc(sem("pick_ready"), 1)
                pick_gates(cur[:, 0:T, :], cur[:, T:2 * T, :])

            def gathered_rows(buf, count):
                for h in range(2):
                    dve.wait_ge(sem("gathered"), count + h + 1)
                    dve.tensor_tensor(buf[:, 4 * h:4 * h + 4, :], bank[6 + h][:].rearrange("p (c s) -> p c s", c=4),
                                      g2[:, 4 * h:4 * h + 4].unsqueeze(2).broadcast_to([P, 4, P]),
                                      ALU.mult).then_inc(sem("xs_ready"), 1)

            gathered_rows(xsT[0], 0)
            dve.wait_ge(sem("gate_ready"), 1)
            pick_gates(table[:, 0:T, 0:2], table[:, T:2 * T, 0:2])
            for c in range(1, PASSES):
                ins = dve.tensor_scalar(table[:, 0:T, c * E:(c + 1) * E], posn[:], -1.0 - c * SLOTS, None, ALU.add)
            ahead(ins, "added")
            dve.wait_ge(sem("gates_ready"), PASSES - 1)
            dve.wait_ge(sem("count_done"), 1)
            ahead(dve.tensor_reduce(most[:], bank[5][:, 0:E], AX.X, ALU.max), "up_read")
            dve.tensor_scalar(flag[:], most[:], float(SLOTS), None, ALU.is_gt).then_inc(sem("flag_ready"), 1)
            from_aside(dve, 0)

            def pair_steps(n, i, pair):
                p = n * 2 + i
                first = AHEAD + p * CPP + FRONT
                aside_used(dve, 0)
                for h in range(2):
                    if h:
                        dve.wait_ge(ring_read, first + CPP // 3)
                    else:
                        dve.wait_ge(sem("half_done"), p * 3 + 1)
                    dve.tensor_scalar(gt[:, h * HALF:(h + 1) * HALF], bank[h][:], LIMIT, None, ALU.min)\
                       .then_inc(sem("gt_ready"), 1)
                dve.wait_ge(sem("sg_ready"), p + 1)
                dve.tensor_tensor(gt, gt, sg, ALU.mult).then_inc(sem("gated"), 1)
                dve.wait_ge(sem("gtT_done"), p + 1)
                dve.wait_ge(sem("gathered"), p * 2 + 2)
                choose(p, i, pair)
                aside_used(dve, 1)
                for h in range(2):
                    if h:
                        dve.wait_ge(ring_read, first + 2 * CPP // 3)
                    else:
                        dve.wait_ge(sem("half_done"), p * 3 + 2)
                    dve.tensor_scalar(up[:, h * HALF:(h + 1) * HALF], bank[2 + h][:], LIMIT, -LIMIT, ALU.min,
                                      ALU.max).then_inc(sem("up_read"), 1)
                dve.wait_ge(sem("gated"), AHEAD + p + 1)
                for h in range(2):
                    dve.wait_ge(sem("up_read"), AHEAD + p * 2 + h + 1)
                    r = slice(h * HALF, (h + 1) * HALF)
                    dve.scalar_tensor_tensor(up[:, r], up[:, r], 1.0, gt[:, r], ALU.add, ALU.mult).then_inc(sem("act_ready"), 1)
                aside_used(dve, 2)
                gathered_rows(xsT[1 - i], p * 2 + 2)
                dve.wait_ge(ring_read, first + CPP)
                dve.wait_ge(sem("combined"), AHEAD + p * 4)
                dve.tensor_copy(yy[:, HALF:D], bank[5][:]).then_inc(sem("y1_ready"), 1)
                dve.wait_ge(sem("added"), AHEAD + p * 4)
                for nh in range(NH):
                    for t in range(T):
                        r = slice(nh * HALF, (nh + 1) * HALF)
                        dve.wait_ge(sem("combined"), AHEAD + p * 4 + T * nh + t + 1)
                        dve.tensor_tensor(x[:, t, r], bank[6 - 2 * nh + t][:], x[:, t, r], ALU.add).then_inc(sem("added"), 1)

            over = overflowed(dve)
            with dve.Fori(0, BODIES) as n:
                for i in range(2):
                    pair_steps(n, i, n * 2 + i)
            with dve.If(over > 0):
                with dve.Fori(1, PASSES) as c:
                    with dve.Fori(0, BODIES) as n:
                        for i in range(2):
                            pair_steps(c * BODIES + n, i, n * 2 + i)
                dve.wait_ge(sem("added"), AHEAD + PASSES * PAIRS * 4)
            dve.wait_ge(sem("added"), AHEAD + PAIRS * 4)
            for t in range(T):
                mean_of_halves(msc, ssc, t, "normf", T * (NH - 1) + t + 1)
            for t in range(T):
                dve.wait_ge(sem("normf_rstd"), t + 1)
                for nh in range(NH):
                    dve.wait_ge(sem("normf_wide"), nh + 1)
                    r = slice(nh * HALF, (nh + 1) * HALF)
                    dve.scalar_tensor_tensor(x[:, t, r], x[:, t, r], rstdc[:, t:t + 1], bank[2 + nh][:], ALU.mult,
                                             ALU.mult).then_inc(sem("out_ready"), 1)


_INS = ["x", "norm1_g", "w_in", "hgrn_lb", "hgrn_norm_g", "pool_w", "pool_scale", "w_out", "norm2_g", "router_w",
        "router_b", "w_gate", "b_gate", "w_up", "b_up", "w_down", "b_down", "norm_f_g"]


def kernel(**inputs):
    import concourse.bacc as _bacc
    from concourse.bass_utils import run_bass_kernel_spmd as _run

    nc = _bacc.Bacc("TRN2", target_bir_lowering=False, num_devices=1)
    arrays, args = {}, {}
    for name in _INS:
        arrays[f"in_{name}"] = np.ascontiguousarray(inputs[name])
    arrays["in_consts"] = layer_constants()[0]
    for name, a in arrays.items():
        args[name[3:]] = nc.dram_tensor(name, a.shape, mybir.dt.from_np(a.dtype), kind="ExternalInput").ap()
    out = nc.dram_tensor("out", (1, SEQ, D), F32, kind="ExternalOutput").ap()
    hybrid_hgrn2_pool_moe(nc, args, out)
    r = _run(nc, [arrays], core_ids=[0])
    return r.results[0]["out"]
```
